# Optimizing a Trainium2 kernel written in Bass

```python
import jax, jax.numpy as jnp
from jax import lax
import numpy as np

D_MODEL = 1024
BATCH = 1
SEQ = 512
DEPTH = 1
DEC_BATCH = 8
DEC_SEQ = 1
PAST_LEN = 1024
PAGE_SIZE = 128

MIX_WIDTH = D_MODEL
MLA_WIDTH = D_MODEL // 2
POOL_WIDTH = MIX_WIDTH - MLA_WIDTH
MLA_HEADS = 4
V_HEAD = MLA_WIDTH // MLA_HEADS
QK_NOPE = 128
QK_ROPE = 64
Q_LORA = 384
KV_LORA = 256
MLA_SCALE = (QK_NOPE + QK_ROPE) ** -0.5
Q_BLOCK = 128
POOL_WINDOWS = (2, 4, 8, 16)
POOL_GROUPS = len(POOL_WINDOWS)
POOL_GROUP_W = POOL_WIDTH // POOL_GROUPS
POOL_STATE = max(POOL_WINDOWS) - 1
N_MEM = 256
MEM_HEADS = 4
MEM_HEAD_DIM = D_MODEL // MEM_HEADS
MEM_SCALE = MEM_HEAD_DIM ** -0.5
D_FF = -(-8 * D_MODEL // (3 * 256)) * 256
IN_WIDTH = Q_LORA + KV_LORA + QK_ROPE + POOL_WIDTH
ROPE_THETA = 10000.0
EPS = 1e-6

kernel_name = "hymba_mla_pool_memxattn_step"

def rmsnorm(x, g):
    xf = x.astype(jnp.float32)
    y = xf * lax.rsqrt(jnp.mean(xf * xf, -1, keepdims=True) + EPS)
    return (y * g.astype(jnp.float32)).astype(x.dtype)

def rope_tables(pos):
    half = QK_ROPE // 2
    inv = jnp.power(ROPE_THETA, -(jnp.arange(half, dtype=jnp.float32) / half))
    ang = pos.astype(jnp.float32)[:, None] * inv[None, :]
    return jnp.cos(ang), jnp.sin(ang)

def apply_rope(x, cos, sin):
    xf = x.astype(jnp.float32)
    x1, x2 = xf[..., : QK_ROPE // 2], xf[..., QK_ROPE // 2:]
    return jnp.concatenate([x1 * cos - x2 * sin, x1 * sin + x2 * cos], -1).astype(x.dtype)

def mixer_inputs(h, pos, w_in, q_norm, w_uq, kv_norm, w_uk):
    B, T = h.shape[:2]
    u = h @ w_in
    i0, i1, i2 = Q_LORA, Q_LORA + KV_LORA, Q_LORA + KV_LORA + QK_ROPE
    cq, ckv, kr, up = u[..., :i0], u[..., i0:i1], u[..., i1:i2], u[..., i2:]
    q = (rmsnorm(cq, q_norm) @ w_uq).reshape(B, T, MLA_HEADS, QK_NOPE + QK_ROPE)
    cos, sin = rope_tables(pos)
    q_rope = apply_rope(q[..., QK_NOPE:], cos[:, None, :], sin[:, None, :])
    q_lat = jnp.einsum('bthn,rhn->bthr', q[..., :QK_NOPE], w_uk)
    c = rmsnorm(ckv, kv_norm)
    k_rope = apply_rope(kr, cos, sin)
    return q_lat, q_rope, c, k_rope, up

def mla_scores(q_lat, q_rope, c, k_rope):
    s = jnp.einsum('bthr,bsr->bhts', q_lat, c).astype(jnp.float32)
    s = s + jnp.einsum('bthp,bsp->bhts', q_rope, k_rope).astype(jnp.float32)
    return s * MLA_SCALE

def mla_attend_prompt(q_lat, q_rope, c, k_rope):
    B, T = q_lat.shape[:2]
    nb = T // Q_BLOCK
    kpos = jnp.arange(T)
    ql = q_lat.reshape(B, nb, Q_BLOCK, MLA_HEADS, KV_LORA).transpose(1, 0, 2, 3, 4)
    qr = q_rope.reshape(B, nb, Q_BLOCK, MLA_HEADS, QK_ROPE).transpose(1, 0, 2, 3, 4)
    qpos = jnp.arange(T).reshape(nb, Q_BLOCK)

    def block(args):
        qlb, qrb, qp = args
        s = mla_scores(qlb, qrb, c, k_rope)
        s = jnp.where(kpos[None, :] <= qp[:, None], s, -jnp.inf)
        p = jax.nn.softmax(s, -1).astype(c.dtype)
        return jnp.einsum('bhts,bsr->bthr', p, c)

    o = lax.map(block, (ql, qr, qpos))
    return o.transpose(1, 0, 2, 3, 4).reshape(B, T, MLA_HEADS, KV_LORA)

def mla_attend_sample(q_lat, q_rope, c_past, kr_past, c_new, kr_new):
    T = q_lat.shape[1]
    P = c_past.shape[1]
    s_past = mla_scores(q_lat, q_rope, c_past, kr_past)
    s_new = mla_scores(q_lat, q_rope, c_new, kr_new)
    s_new = jnp.where(jnp.tril(jnp.ones((T, T), bool)), s_new, -jnp.inf)
    p = jax.nn.softmax(jnp.concatenate([s_past, s_new], -1), -1).astype(c_new.dtype)
    return (jnp.einsum('bhts,bsr->bthr', p[..., :P], c_past)
            + jnp.einsum('bhts,bsr->bthr', p[..., P:], c_new))

def pool_mix(xp, prev, pos0, w_pool, pool_scale):
    B, T, C = xp.shape
    P = prev.shape[1]
    buf = jnp.concatenate([prev, xp], 1)
    cs = jnp.concatenate([jnp.zeros((B, 1, C), jnp.float32),
                          jnp.cumsum(buf.astype(jnp.float32), 1)], 1)
    pos = pos0 + jnp.arange(T)
    hi = cs[:, P + 1:P + 1 + T]
    xf = xp.astype(jnp.float32)
    outs = []
    for g, w in enumerate(POOL_WINDOWS):
        sl = slice(g * POOL_GROUP_W, (g + 1) * POOL_GROUP_W)
        lo = cs[:, P + 1 - w:P + 1 - w + T, sl]
        cnt = jnp.minimum(w, pos + 1).astype(jnp.float32)[None, :, None]
        outs.append((hi[..., sl] - lo) / cnt - xf[..., sl])
    m = jnp.stack(outs, 2).astype(xp.dtype)
    y = jnp.einsum('btgc,gcd->btgd', m, w_pool).reshape(B, T, C) * pool_scale
    return y, buf[:, -POOL_STATE:]

def mixer_out(o_lat, pool_y, w_uv, w_out):
    B, T = o_lat.shape[:2]
    o_mla = jnp.einsum('bthr,rhv->bthv', o_lat, w_uv).reshape(B, T, MLA_WIDTH)
    return jnp.concatenate([o_mla, pool_y], -1) @ w_out

def mem_kv(mem, mem_norm, w_mk, w_mv):
    B = mem.shape[0]
    m = rmsnorm(mem, mem_norm)
    return ((m @ w_mk).reshape(B, N_MEM, MEM_HEADS, MEM_HEAD_DIM),
            (m @ w_mv).reshape(B, N_MEM, MEM_HEADS, MEM_HEAD_DIM))

def mem_attend(h, mk, mv, w_xq, w_xo):
    B, T = h.shape[:2]
    q = (h @ w_xq).reshape(B, T, MEM_HEADS, MEM_HEAD_DIM)
    s = jnp.einsum('bthd,bmhd->bhtm', q, mk).astype(jnp.float32) * MEM_SCALE
    p = jax.nn.softmax(s, -1).astype(mv.dtype)
    o = jnp.einsum('bhtm,bmhd->bthd', p, mv).reshape(B, T, MEM_HEADS * MEM_HEAD_DIM)
    return o @ w_xo

def swiglu(h, w_gate, w_up, w_down):
    return (jax.nn.silu(h @ w_gate) * (h @ w_up)) @ w_down

def setup_inputs(seed: int = 0) -> dict:
    key = jax.random.key(seed)
    ks = iter(jax.random.split(key, 40))
    f32 = jnp.float32

    def nrm(shape, scale=1.0):
        return jax.random.normal(next(ks), shape, f32) * scale

    def gain(shape):
        return 1.0 + 0.05 * nrm(shape)

    n_pages = PAST_LEN // PAGE_SIZE
    n_used = DEC_BATCH * n_pages
    n_phys = n_used + max(1, n_used // 4)
    page_table = jax.random.permutation(next(ks), n_phys)[:n_used].reshape(DEC_BATCH, n_pages).astype(jnp.int32)
    L = DEPTH
    return {
        "x_prompt": nrm((BATCH, SEQ, D_MODEL)),
        "x_sample": nrm((DEC_BATCH, DEC_SEQ, D_MODEL)),
        "mem_prompt": nrm((BATCH, N_MEM, D_MODEL)),
        "cache_kv_latent": nrm((L, n_phys, PAGE_SIZE, KV_LORA)),
        "cache_k_rope": nrm((L, n_phys, PAGE_SIZE, QK_ROPE)),
        "cache_pool": nrm((L, DEC_BATCH, POOL_STATE, POOL_WIDTH)),
        "cache_mem_k": nrm((L, DEC_BATCH, N_MEM, MEM_HEADS, MEM_HEAD_DIM)),
        "cache_mem_v": nrm((L, DEC_BATCH, N_MEM, MEM_HEADS, MEM_HEAD_DIM)),
        "page_table": page_table,
        "norm_mix": gain((L, D_MODEL)),
        "w_in": nrm((L, D_MODEL, IN_WIDTH), D_MODEL ** -0.5),
        "q_norm": gain((L, Q_LORA)),
        "w_uq": nrm((L, Q_LORA, MLA_HEADS * (QK_NOPE + QK_ROPE)), Q_LORA ** -0.5),
        "kv_norm": gain((L, KV_LORA)),
        "w_uk": nrm((L, KV_LORA, MLA_HEADS, QK_NOPE), KV_LORA ** -0.5),
        "w_uv": nrm((L, KV_LORA, MLA_HEADS, V_HEAD), KV_LORA ** -0.5),
        "w_pool": nrm((L, POOL_GROUPS, POOL_GROUP_W, POOL_GROUP_W), POOL_GROUP_W ** -0.5),
        "pool_scale": gain((L, POOL_WIDTH)),
        "w_out": nrm((L, MIX_WIDTH, D_MODEL), MIX_WIDTH ** -0.5),
        "norm_x": gain((L, D_MODEL)),
        "mem_norm": gain((L, D_MODEL)),
        "w_xq": nrm((L, D_MODEL, MEM_HEADS * MEM_HEAD_DIM), D_MODEL ** -0.5),
        "w_mk": nrm((L, D_MODEL, MEM_HEADS * MEM_HEAD_DIM), D_MODEL ** -0.5),
        "w_mv": nrm((L, D_MODEL, MEM_HEADS * MEM_HEAD_DIM), D_MODEL ** -0.5),
        "w_xo": nrm((L, MEM_HEADS * MEM_HEAD_DIM, D_MODEL), D_MODEL ** -0.5),
        "norm_ffn": gain((L, D_MODEL)),
        "w_gate": nrm((L, D_MODEL, D_FF), D_MODEL ** -0.5),
        "w_up": nrm((L, D_MODEL, D_FF), D_MODEL ** -0.5),
        "w_down": nrm((L, D_FF, D_MODEL), D_FF ** -0.5),
        "norm_final": gain((D_MODEL,)),
    }

def reference(x_prompt, x_sample, mem_prompt, cache_kv_latent, cache_k_rope, cache_pool,
              cache_mem_k, cache_mem_v, page_table, norm_mix, w_in, q_norm, w_uq, kv_norm,
              w_uk, w_uv, w_pool, pool_scale, w_out, norm_x, mem_norm, w_xq, w_mk, w_mv,
              w_xo, norm_ffn, w_gate, w_up, w_down, norm_final):
    B, T = x_prompt.shape[:2]
    DB, TS = x_sample.shape[:2]
    past = page_table.shape[1] * PAGE_SIZE
    pos_p = jnp.arange(T)
    pos_s = past + jnp.arange(TS)
    xp, xs = x_prompt, x_sample
    kvl_p, kr_p, pool_p, mk_p, mv_p = [], [], [], [], []
    kvl_s, kr_s, pool_s = [], [], []
    for l in range(DEPTH):
        ql, qr, c, kr, up = mixer_inputs(rmsnorm(xp, norm_mix[l]), pos_p, w_in[l], q_norm[l],
                                         w_uq[l], kv_norm[l], w_uk[l])
        o_lat = mla_attend_prompt(ql, qr, c, kr)
        py, pst = pool_mix(up, jnp.zeros((B, POOL_STATE, POOL_WIDTH), up.dtype), 0,
                           w_pool[l], pool_scale[l])
        xp = xp + mixer_out(o_lat, py, w_uv[l], w_out[l])
        mk, mv = mem_kv(mem_prompt, mem_norm[l], w_mk[l], w_mv[l])
        xp = xp + mem_attend(rmsnorm(xp, norm_x[l]), mk, mv, w_xq[l], w_xo[l])
        xp = xp + swiglu(rmsnorm(xp, norm_ffn[l]), w_gate[l], w_up[l], w_down[l])
        kvl_p.append(c); kr_p.append(kr); pool_p.append(pst); mk_p.append(mk); mv_p.append(mv)
        ql, qr, c_n, kr_n, us = mixer_inputs(rmsnorm(xs, norm_mix[l]), pos_s, w_in[l], q_norm[l],
                                             w_uq[l], kv_norm[l], w_uk[l])
        c_past = cache_kv_latent[l][page_table].reshape(DB, past, KV_LORA)
        kr_past = cache_k_rope[l][page_table].reshape(DB, past, QK_ROPE)
        o_lat = mla_attend_sample(ql, qr, c_past, kr_past, c_n, kr_n)
        sy, sst = pool_mix(us, cache_pool[l], past, w_pool[l], pool_scale[l])
        xs = xs + mixer_out(o_lat, sy, w_uv[l], w_out[l])
        xs = xs + mem_attend(rmsnorm(xs, norm_x[l]), cache_mem_k[l], cache_mem_v[l], w_xq[l], w_xo[l])
        xs = xs + swiglu(rmsnorm(xs, norm_ffn[l]), w_gate[l], w_up[l], w_down[l])
        kvl_s.append(c_n); kr_s.append(kr_n); pool_s.append(sst)
    y_prompt = rmsnorm(xp, norm_final)
    y_sample = rmsnorm(xs, norm_final)
    return (y_prompt, y_sample,
            jnp.stack(kvl_p), jnp.stack(kr_p), jnp.stack(pool_p), jnp.stack(mk_p), jnp.stack(mv_p),
            jnp.stack(kvl_s), jnp.stack(kr_s), jnp.stack(pool_s))


_drawn_inputs = setup_inputs


def setup_inputs(seed=0):
    import zlib

    import numpy as np

    out = dict(_drawn_inputs(seed))
    spreads = {}
    factors = {'cache_k_rope': 3.086, 'q_norm': 8.0, 'norm_x': 8.0}
    for name, (base, spread) in spreads.items():
        noise = np.random.default_rng([zlib.crc32(name.encode()), seed]).standard_normal(out[name].shape)
        drawn = base * np.exp(spread * noise) if base else spread * noise
        out[name] = __import__('jax').numpy.asarray(drawn.astype(out[name].dtype))
    for name, factor in factors.items():
        out[name] = (out[name] * factor).astype(out[name].dtype)
    return out
```

```python
from contextlib import ExitStack

import numpy as np
import concourse.bass as bass
from concourse import mybir

F32 = mybir.dt.float32
F32R = mybir.dt.float32r
I32 = mybir.dt.int32
ALU = mybir.AluOpType
ACT = mybir.ActivationFunctionType
AX = mybir.AxisListType.X

P = 128
D = 1024
KD = D // P
TP = 512
NB = 8
T = TP + NB
TH = T // 2
HALF = [(0, TH), (TH, T)]
PROMPT = [(0, TH), (TH, TP)]
NH = 4
QL, KVL, RP, PW = 384, 256, 64, 512
NOPE = 128
QH = NOPE + RP
KQ = QL // P
PAGE, NPG = 128, 8
NPHYS = 80
TPP = PAGE * NPG // P
NMEM = 256
MD = 256
FF = 2816
NF = FF // P
WINDOWS = (2, 4, 8, 16)
NST = 15
EPS = 1e-6
MLA_SCALE = float(QH) ** -0.5
MEM_SCALE = float(MD) ** -0.5
BIG = -3.0e38

G_MIX, G_X, G_FFN, G_FIN, G_MEM, G_PS, G_Q, G_KV = 0, 8, 16, 24, 32, 40, 44, 47
NG = 49
NC_CONST = 3 * P + 2 * T + 4 * 16

RAW, SPL = 2, 3
RING = 6

S_IN = 0
S_UQ = S_IN + 10
S_POOL = S_UQ + 3
S_UV = S_POOL + 1
S_OUT = S_UV + 1
S_MK = S_OUT + KD
S_MV = S_MK + KD
S_XQ = S_MV + KD
S_XO = S_XQ + KD
S_FFN = S_XO + KD
S_DOWN = S_FFN + 2 * NF
DPART = [(0, 8), (8, 16), (16, 22)]
NSLOT = S_DOWN + 3 * KD


class Order:

    def __init__(self, keys):
        self.at = {k: n for n, k in enumerate(keys)}
        assert len(self.at) == len(keys)

    def __getitem__(self, key):
        return self.at[key]


def units():
    return [(h, i) for h in range(NH) for i in range(4)]


def bank_order():
    o = [("gain",), ("xs",)] + [("xt", c) for c in range(KD)] + [("cp",)] + [("wuk", h) for h in range(NH)]
    for m in range(10):
        o += [("in", m, f) for f in (0, 1)]
        if m == 0:
            o += [("ssq", "n1", f) for f in (0, 1)]
        if m == 6:
            o += [("rotk", f) for f in (0, 1)]
        if m == 7:
            o += [("ssq", "nq", f) for f in (0, 1)]
        if m == 8:
            o += [("ssq", "nkv", f) for f in (0, 1)]
    o += [("un", h, f) for h in range(NH) for f in (0, 1)]
    o += [("ur", p, f) for p in (0, 1) for f in (0, 1)]
    for g in range(4):
        o += [("py", g, f) for f in (0, 1)]
        if g < 2:
            o += [("rotq", g, f) for f in (0, 1)]
    o += [("ct", t) for t in range(4)] + [("kt",), ("smp",), ("us",), ("ut",), ("qls",)]
    o += [("ql", 0, 0), ("ql", 0, 1), ("s", 0, 0), ("s", 0, 1), ("snew",)]
    us = units()
    for n, (h, i) in enumerate(us):
        o += [("pt", h, i)]
        if i == 0 and h:
            o += [("uv", h - 1)]
        if n + 2 < len(us):
            o += [("s",) + us[n + 2]]
        if i == 1 and h + 1 < NH:
            o += [("ql", h + 1, 0), ("ql", h + 1, 1)]
        if i == 3:
            o += [("pv", h, 0), ("pv", h, 1)]
    o += [("uv", NH - 1)]
    o += [("tb", b, k) for b in range(NB) for k in range(5)]
    o += [("mxt",), ("mxb",), ("tot",), ("uvs",)]
    for m in range(KD):
        o += [("o", m, f) for f in (0, 1)]
        if m == 1:
            o += [("mt", k) for k in range(4)]
    for j in range(16):
        o += [("mm", j)]
        if j >= 2 and j % 2 == 0:
            o += [("mn", j // 2 - 1)]
    o += [("mn", 7)]
    for m in range(KD):
        o += [("xq", m, f) for f in (0, 1)]
        if m == 0:
            o += [("ssq", "nx", f) for f in (0, 1)]
    o += [("qt", 0), ("qt", 1), ("cs", 0, 0), ("cs", 0, 1)]
    for h in range(NH):
        if h + 1 < NH:
            o += [("cs", h + 1, 0), ("cs", h + 1, 1)]
        o += [("cpt", h, 0), ("cpt", h, 1), ("qb", 2 * h, 0), ("qb", 2 * h, 1)]
        o += [("cpv", h, 0), ("cpv", h, 1), ("qb", 2 * h + 1, 0), ("qb", 2 * h + 1, 1)]
    o += [("cmxt",), ("cmxb",), ("ctot",)]
    o += [("xo", m, f) for m in range(KD) for f in (0, 1)]
    for j in range(NF):
        o += [("g", j, 0), ("g", j, 1), ("u", j, 0), ("u", j, 1)]
        if j == 0:
            o += [("ssq", "nf", f) for f in (0, 1)]
    o += [("d", m, f) for m in range(KD) for f in (0, 1)]
    o += [("ssq", "nz", f) for f in (0, 1)]
    o += [("y", t, k) for t in range(5) for k in (0, 1)]
    return o


def val_order():
    o = [("gT",), ("xs1",)] + [("x1", c) for c in range(KD)] + [("cpT",)]
    for m in range(10):
        if m == 0:
            o += [("ms", "n1", f) for f in (0, 1)]
        if m < 3:
            o += [("cq", m, f) for f in (0, 1)]
        elif m < 5:
            o += [("ckv", m - 3, f) for f in (0, 1)]
        elif m == 5:
            o += [("krx", f) for f in (0, 1)]
        else:
            o += [("up", m - 6, f) for f in (0, 1)]
        if m == 6:
            o += [("kr", f) for f in (0, 1)]
        if m == 7:
            o += [("ms", "nq", f) for f in (0, 1)]
        if m == 8:
            o += [("ms", "nkv", f) for f in (0, 1)]
            o += [("c", r, f) for f in (0, 1) for r in (0, 1)]
    o += [("qn", h, f) for h in range(NH) for f in (0, 1)]
    o += [("qx", p, f) for p in (0, 1) for f in (0, 1)]
    o += [("pm", g) for g in range(4)]
    o += [("qr", p, f) for p in (0, 1) for f in (0, 1)]
    o += [("qls",), ("sprod",)]
    us = units()
    o += [("negm",) + us[0]]
    for n, u in enumerate(us):
        o += [("negm",) + v for v in us[n + 1:n + 2]] + [("pn",) + u]
    o += [("mx",), ("diag",), ("dif",), ("sum",), ("pnorm",), ("osum",)]
    for m in range(KD):
        o += [("xo1", m, f) for f in (0, 1)]
        if m == 1:
            o += [("ms", "mem"), ("memn",)]
    o += [("ms", "nx", f) for f in (0, 1)]
    for m in range(KD):
        o += [("xq", m, f) for f in (0, 1)]
    o += [("cnegm", 0)]
    for h in range(NH):
        o += [("cnegm", v) for v in range(h + 1, min(h + 2, NH))] + [("cpn", h)]
    o += [("cmx",), ("cdiag",), ("cdif",), ("csum",), ("cpnorm",)]
    o += [("xo2", m, f) for m in range(KD) for f in (0, 1)]
    o += [("ms", "nf", f) for f in (0, 1)]
    for j in range(NF):
        o += [("gv", j, 0), ("gv", j, 1), ("h", j, 0), ("h", j, 1)]
    o += [("xo3", m, f) for m in range(KD) for f in (0, 1)]
    o += [("ms", "nz", f) for f in (0, 1)]
    o += [("yT", m, f) for f in (0, 1) for m in range(KD)]
    return o


def split_order():
    o = [("x1", c) for c in range(KD)] + [("xs1",)] + [("wuk", h) for h in range(NH)]
    for m in range(10):
        if m < 3:
            o += [("cq", m, f) for f in (0, 1)]
        if m == 6:
            o += [("kr", f) for f in (0, 1)]
        if m == 8:
            o += [("c", r, f) for f in (0, 1) for r in (0, 1)]
    o += [("qn", h, f) for h in range(NH) for f in (0, 1)]
    for g in range(4):
        o += [("pm", g)]
    for g in range(4):
        o += [("py", g, f) for f in (0, 1)]
        if g < 2:
            o += [("qr", g, f) for f in (0, 1)]
    o += [("cn", t) for t in range(4)]
    o += [("ql", 0, 0), ("ql", 0, 1)]
    for h, i in units():
        o += [("pt", h, i)]
        if i == 0 and h:
            o += [("uv", h - 1)]
        if i == 1 and h + 1 < NH:
            o += [("ql", h + 1, 0), ("ql", h + 1, 1)]
        if i == 3:
            o += [("pv", h, 0), ("pv", h, 1)]
    o += [("uv", NH - 1), ("osum",), ("uvs",)]
    for m in range(KD):
        o += [("xo1", m, f) for f in (0, 1)]
        if m == 1:
            o += [("mt", k) for k in range(4)]
    for j in range(16):
        if j < 8:
            o += [("mm", j)]
        if j >= 2 and j % 2 == 0 and j // 2 - 1 >= 4:
            o += [("mn", j // 2 - 1)]
    o += [("mn", 7)]
    o += [("xq", m, f) for m in range(KD) for f in (0, 1)]
    for h in range(NH):
        o += [("cpt", h, 0), ("cpt", h, 1), ("cpv", h, 0), ("cpv", h, 1)]
    o += [("co",)]
    o += [("xo2", m, f) for m in range(KD) for f in (0, 1)]
    o += [("h", j, f) for j in range(NF) for f in (0, 1)]
    return o


ROOTS = ["n1", "nq", "nkv", "mem", "nx", "nf", "nz"]


def in_value(m, f):
    if m < 3:
        return ("cq", m, f)
    if m < 5:
        return ("ckv", m - 3, f)
    return ("krx", f) if m == 5 else ("up", m - 6, f)


BY_LOW = ("wuk", "py", "ql", "pt", "uv", "pv", "uvs", "mt", "cpt", "cpv")
BY_VALUE = {
    "ssq": lambda norm, f: ("ms", norm, f),
    "gain": lambda: ("gT",), "xs": lambda: ("xs1",), "xt": lambda c: ("x1", c), "cp": lambda: ("cpT",),
    "in": in_value, "un": lambda h, f: ("qn", h, f), "ur": lambda p, f: ("qx", p, f), "qls": lambda: ("qls",),
    "o": lambda m, f: ("xo1", m, f), "xq": lambda m, f: ("xq", m, f), "xo": lambda m, f: ("xo2", m, f),
    "g": lambda j, f: ("gv", j, f), "d": lambda m, f: ("xo3", m, f),
}


def build(nc, a, consts, outs):
    (y_p, y_s, o_kvp, o_krp, o_poolp, o_mk, o_mv, o_kvs, o_krs, o_pools) = outs
    BANK, VAL, SPLIT = Order(bank_order()), Order(val_order()), Order(split_order())
    ctx = ExitStack()
    with ctx:
        base = -(-nc.sbuf_base // 64) * 64
        RB = T * 4
        where = {"at": base}

        def take(n):
            at = where["at"]
            where["at"] = at + -(-n // 32) * 32
            assert where["at"] <= nc.sbuf_usable_end, where["at"]
            return at

        def at(name, shape, dt, offset):
            return nc.alloc_sbuf_tensor_at(name, [P] + shape, dt, offset=offset)

        def keep(name, shape, dt=F32):
            return at(name, shape, dt, take(4 * int(np.prod(shape))))

        xT = keep("xT", [KD, T])
        wraw = keep("wraw", [RAW, 1024])
        whi = keep("whi", [SPL, 1024], F32R)
        wlo = keep("wlo", [SPL, 1024], F32R)
        ident = keep("ident", [P])
        perm = keep("perm", [P])
        mask = keep("mask", [P])
        rcnt = keep("rcnt", [4, 16])
        ones = keep("ones", [P])
        gT = keep("gT", [64])
        rstd = keep("rstd", [T])
        rstd_q = keep("rstd_q", [T])
        acc = keep("acc", [T])
        sq = keep("sq", [TH])
        tmp = keep("tmp", [4, TH])
        qls = keep("qls", [2, NH, NB])
        stat = keep("stat", [4, 2])
        cstat = keep("cstat", [4, 2, 4])
        mem_ss = keep("mem_ss", [4])
        cols = keep("cols", [8, NB, NH])
        diag = keep("diag", [NB * NH])
        osv = keep("osv", [2, NH, NB])
        ps_ = keep("ps_", [4, NB])
        page_ids = keep("page_ids", [NB * NPG], I32)

        b0 = take(16 * RB)
        B_hi = at("B_hi", [KD, T], F32R, b0)
        B_lo = at("B_lo", [KD, T], F32R, b0 + KD * RB)
        a0 = take(16 * RB)
        A_hi = at("A_hi", [KD, T], F32R, a0)
        A_lo = at("A_lo", [KD, T], F32R, a0 + KD * RB)
        g0 = where["at"]
        g1 = nc.sbuf_usable_end

        where["at"] = g0
        rope_c = keep("rope_c", [T])
        rope_s = keep("rope_s", [T])
        cT = keep("cT", [2, T])
        kr = keep("kr", [T])
        cT_hi = keep("cT_hi", [2, TP], F32R)
        cT_lo = keep("cT_lo", [2, TP], F32R)
        kr_hi = keep("kr_hi", [TP], F32R)
        kr_lo = keep("kr_lo", [TP], F32R)
        cn_hi = keep("cn_hi", [4, KVL], F32R)
        cn_lo = keep("cn_lo", [4, KVL], F32R)
        wuk_hi = keep("wuk_hi", [NH, KVL], F32R)
        wuk_lo = keep("wuk_lo", [NH, KVL], F32R)
        cp_T = at("cp_T", [4, NB * NST], F32, a0 + 4 * RB)
        o_cq = take(6 * RB)
        cqg_hi = at("cqg_hi", [3, T], F32R, o_cq)
        cqg_lo = at("cqg_lo", [3, T], F32R, o_cq + 3 * RB)
        PT_hi = at("PT_hi", [4, TP], F32R, o_cq)
        prob = at("prob", [2, TP], F32, o_cq + 4 * TP * 4)
        o_ring = take(20480)
        c_ring = at("c_ring", [2, TPP, KVL], F32, o_ring)
        r_ring = at("r_ring", [2, TPP, RP], F32, o_ring + 16384)
        x_nat = at("x_nat", [5, D], F32, o_ring)
        up = at("up", [4, NST + T], F32, o_ring)
        ws1 = at("ws1", [NST + T], F32, o_ring + 8576)
        ws2 = at("ws2", [NST + T], F32, o_ring + 10720)
        pm = at("pm", [T], F32, o_ring + 12864)
        o_ol = take(4 * RB)
        ol_hi = at("ol_hi", [2, TP], F32R, o_ol)
        ol_lo = at("ol_lo", [2, TP], F32R, o_ol + 2 * TP * 4)
        cq = at("cq", [3, T], F32, o_ol)
        qx = at("qx", [2, T], F32, o_ol)
        rstd_kv = at("rstd_kv", [T], F32, o_ol + 2 * RB)
        krx = at("krx", [T], F32, o_ol + 3 * RB)
        o_b1, o_b2, o_b3 = b0, b0 + 4 * RB, b0 + 12 * RB
        ql_hi = at("ql_hi", [2, TP], F32R, o_b1)
        ql_lo = at("ql_lo", [2, TP], F32R, o_b1 + 2 * TP * 4)
        pm_hi = [at(f"pm_hi{g}", [T], F32R, (o_b1, o_b1, o_b3, o_b3)[g] + 2 * (g % 2) * RB) for g in range(4)]
        pm_lo = [at(f"pm_lo{g}", [T], F32R, (o_b1, o_b1, o_b3, o_b3)[g] + (2 * (g % 2) + 1) * RB) for g in range(4)]
        qr_hi = at("qr_hi", [NH, T], F32R, o_b2)
        qr_lo = at("qr_lo", [NH, T], F32R, o_b2 + 4 * RB)
        PT_lo = at("PT_lo", [4, TP], F32R, o_b3)
        wuk_raw = at("wuk_raw", [2, NH * NOPE], F32, a0)
        gains = at("gains", [P], F32, a0 + 4096)
        cp_nat = at("cp_nat", [PW], F32, a0 + 4096 + 512)
        c_nat = at("c_nat", [4, KVL], F32, o_b3)
        kr_nat = at("kr_nat", [4, RP], F32, o_b3 + 4096)
        smp_nat = at("smp_nat", [KVL + RP], F32, o_b3 + 5120)
        us_nat = at("us_nat", [PW], F32, g0)
        ut_nat = at("ut_nat", [PW], F32, g0 + RB)
        cTs = at("cTs", [2, 2, TPP, P], F32, b0)
        rTs = at("rTs", [2, TPP // 2, P], F32, b0 + 16384)
        Dm = at("Dm", [NB, TPP, NH], F32, b0 + 20480)
        Pm = at("Pm", [NB, TPP, NH], F32, b0 + 21504)
        ols_hi = at("ols_hi", [2, NH, NB], F32R, b0 + 22528)
        ols_lo = at("ols_lo", [2, NH, NB], F32R, b0 + 22784)
        qrs = at("qrs", [NB, 2, NH], F32, take(256))
        where["at"] = g0
        q_hi = keep("q_hi", [KD, TP], F32R)
        q_lo = keep("q_lo", [KD, TP], F32R)
        mT_hi = at("mT_hi", [KD, NMEM], F32R, g0)
        mT_lo = at("mT_lo", [KD, NMEM], F32R, g0 + KD * NMEM * 4)
        m_nat = at("m_nat", [2, D], F32, g0 + 2 * KD * NMEM * 4)
        mkT_hi = keep("mkT_hi", [KD, NMEM], F32R)
        mkT_lo = keep("mkT_lo", [KD, NMEM], F32R)
        mvn_hi = keep("mvn_hi", [2, D], F32R)
        mvn_lo = keep("mvn_lo", [2, D], F32R)
        o_pc = take(14080)
        PTc_hi = at("PTc_hi", [2, TP], F32R, o_pc)
        PTc_lo = at("PTc_lo", [2, TP], F32R, o_pc + 4096)
        kv_nat = at("kv_nat", [2, D], F32, o_pc)
        m_sq = at("m_sq", [2, D], F32, o_pc)
        kv_T = at("kv_T", [4, NMEM], F32, o_pc + 8192)
        q_nat = at("q_nat", [D], F32, o_pc + 8192)
        prod = at("prod", [MD], F32, o_pc + 12288)
        Sc = at("Sc", [NB, 2, NH], F32, o_pc + 13312)
        Dc = at("Dc", [NB, 2, NH], F32, o_pc + 13568)
        Pcs = at("Pcs", [NB, 2, NH], F32, o_pc + 13824)
        K3 = 3
        kv_ring = at("kv_ring", [K3, 2, D], F32, b0)
        Pc = at("Pc", [2, 2, 2, NMEM], F32, b0 + K3 * 8192)
        qcs = at("qcs", [KD, NB], F32, take(256))
        where["at"] = a0
        h_hi = keep("h_hi", [NF, T], F32R)
        h_lo = keep("h_lo", [NF, T], F32R)
        gate = keep("gate", [2, TH])
        sig = keep("sig", [2, TH])
        upv = keep("upv", [2, TH])
        hv = keep("hv", [2, TH])
        yT = at("yT", [KD, T], F32, b0)
        y_nat = at("y_nat", [2, D], F32, b0 + KD * RB)

        ps = ctx.enter_context(nc.psum_tensor("ps", [P, 8, 512], F32))
        accS, accO = ps[:, 6], ps[:, 7]

        def sem(name):
            return ctx.enter_context(nc.semaphore(name))

        bank_full = [sem(f"bank_full{i}") for i in range(RING)]
        bank_free = [sem(f"bank_free{i}") for i in range(RING)]
        w_loaded = [sem(f"w_loaded{i}") for i in range(RAW)]
        w_hi, w_lo = sem("w_hi"), sem("w_lo")
        down_used = sem("down_used")
        val = sem("val")
        hi, lo = sem("hi"), sem("lo")
        root = sem("root")
        sums = sem("sums")
        dve_step, act_step, gp_step = sem("dve_step"), sem("act_step"), sem("gp_step")
        consts_in, gains_in, x_in, wuk_in, cp_in, rope_in, ids_in, mem_in = (
            sem(n) for n in ("consts_in", "gains_in", "x_in", "wuk_in", "cp_in", "rope_in", "ids_in", "mem_in"))
        ones_set, pads_set = sem("ones_set"), sem("pads_set")
        winsum = sem("winsum")
        c_in = [sem(f"c_in{i}") for i in range(2)]
        c_used = [sem(f"c_used{i}") for i in range(2)]
        kv_in = [sem(f"kv_in{i}") for i in range(K3)]
        v_used = sem("v_used")
        mem_sq = sem("mem_sq")
        s_exp, c_exp = sem("s_exp"), sem("c_exp")
        sig_set = sem("sig_set")
        qcs_set = sem("qcs_set")
        stored = sem("stored")
        kv_st = sem("kv_st")
        y_st = [sem(f"y_st{i}") for i in range(2)]

        def gain(row):
            return gT[:, row:row + 1]

        def full(eng, key):
            n = BANK[key]
            eng.wait_ge(bank_full[n % RING], n // RING + 1)
            return ps[:, n % RING]

        own_frees = [0] * RING
        free_count = {}
        for n, key in enumerate(bank_order()):
            if key[0] not in BY_LOW and key[0] not in BY_VALUE:
                own_frees[n % RING] += 1
                free_count[key] = own_frees[n % RING]

        def freed(eng, key):
            if key[0] in BY_LOW:
                eng.wait_ge(lo, SPLIT[key] + 1)
            elif key[0] in BY_VALUE:
                eng.wait_ge(val, VAL[BY_VALUE[key[0]](*key[1:])] + 1)
            else:
                eng.wait_ge(bank_free[BANK[key] % RING], free_count[key])

        def frees(ins, key):
            assert key in free_count
            ins.then_inc(bank_free[BANK[key] % RING], 1)

        w_in, w_uq, w_uv = a["w_in"][0], a["w_uq"][0], a["w_uv"][0]

        def columns(w, c0, k0=0, k1=KD, n=P):
            return w[k0 * P:k1 * P, c0:c0 + n].rearrange("(k p) n -> p k n", p=P)

        slots = []

        def slot(k, n, parts):
            slots.append((k, n, parts))

        in_cols = [0, 128, 256, 384, 512, None, 704, 832, 960, 1088]
        for c0 in in_cols:
            if c0 is None:
                r0 = QL + KVL
                slot(KD, P, [(0, RP, columns(w_in, r0, n=RP)), (RP, RP, columns(w_in, r0, n=RP))])
            else:
                slot(KD, P, [(0, P, columns(w_in, c0))])
        for h0 in (0, 2):
            slot(KQ, 2 * P, [(P * i, P, columns(w_uq, (h0 + i) * QH, 0, KQ)) for i in (0, 1)])
        slot(KQ, 2 * P, [(RP * i, RP, columns(w_uq, i * QH + NOPE, 0, KQ, RP)) for i in range(NH)])
        slot(4, P, [(0, P, a["w_pool"][0].rearrange("g c d -> c g d"))])
        slot(2, PW, [(0, PW, w_uv.rearrange("(k p) h v -> p k (h v)", p=P))])
        for name in ("w_out", "w_mk", "w_mv", "w_xq", "w_xo"):
            for m in range(KD):
                slot(KD, P, [(0, P, columns(a[name][0], m * P))])
        for j in range(NF):
            for name in ("w_gate", "w_up"):
                slot(KD, P, [(0, P, columns(a[name][0], j * P))])
        for m in range(KD):
            for k0, k1 in DPART:
                slot(k1 - k0, P, [(0, P, columns(a["w_down"][0], m * P, k0, k1))])
        assert len(slots) == NSLOT
        landed, count = [], [0] * RAW
        for s, (_, _, parts) in enumerate(slots):
            count[s % RAW] += 16 * len(parts)
            landed.append(count[s % RAW])

        def used(eng, s):
            if s >= S_DOWN:
                m, part = divmod(s - S_DOWN, 3)
                if part == 2:
                    full(eng, ("d", m, 1))
                else:
                    eng.wait_ge(down_used, 2 * m + part + 1)
            elif s >= S_FFN:
                j, i = divmod(s - S_FFN, 2)
                full(eng, ("gu"[i], j, 1))
            elif s >= S_XO:
                full(eng, ("xo", s - S_XO, 1))
            elif s >= S_XQ:
                full(eng, ("xq", s - S_XQ, 1))
            elif s >= S_MK:
                full(eng, ("mm", s - S_MK))
            elif s >= S_OUT:
                full(eng, ("o", s - S_OUT, 1))
            elif s >= S_UQ:
                full(eng, {S_UQ: ("un", 1, 1), S_UQ + 1: ("un", 3, 1), S_UQ + 2: ("ur", 1, 1),
                           S_POOL: ("py", 3, 1), S_UV: ("uvs",)}[s])
            else:
                full(eng, ("in", s - S_IN, 1))

        def pieces(s):
            n = slots[s][0] * slots[s][1]
            return [(0, n // 2), (n // 2, n)]

        def w(s, k, c0=0, n=P):
            o = k * slots[s][1] + c0
            return whi[:, s % SPL, o:o + n], wlo[:, s % SPL, o:o + n]

        block = ctx.enter_context(nc.Block())

        @block.sync
        def _(sp):
            def load_w(s):
                if s >= RAW:
                    sp.wait_ge(w_lo, 2 * (s - RAW + 1))
                k, n, parts = slots[s]
                view = wraw[:, s % RAW, 0:k * n].rearrange("p (k n) -> p k n", k=k)
                for c0, width, src in parts:
                    sp.dma_start(view[:, :, c0:c0 + width], src).then_inc(w_loaded[s % RAW], 16)

            c = 0
            for t, n in ((ident, P), (perm, P), (mask, P)):
                sp.dma_start(t[:, :], consts[:, c:c + n]).then_inc(consts_in, 16)
                c += n
            row = 0
            for name, n in (("norm_mix", 8), ("norm_x", 8), ("norm_ffn", 8), ("norm_final", 8), ("mem_norm", 8),
                            ("pool_scale", 4), ("q_norm", 3), ("kv_norm", 2)):
                g = a[name] if name == "norm_final" else a[name][0]
                sp.dma_start(gains[row:row + n, :], g.rearrange("(c p) -> c p", p=P)).then_inc(gains_in, 16)
                row += n
            sp.dma_start(x_nat[0:NB, 4, :], a["x_sample"].rearrange("b t d -> (b t) d")).then_inc(x_in, 16)
            for t in range(4):
                sp.dma_start(x_nat[:, t, :], a["x_prompt"][0, t * P:(t + 1) * P, :]).then_inc(x_in, 16)
            load_w(0)
            load_w(1)
            sp.dma_start(wuk_raw[:, :, :], a["w_uk"][0].rearrange("(k p) h n -> p k (h n)", p=P)).then_inc(wuk_in, 16)
            sp.dma_start(cp_nat[0:NB * NST, :], a["cache_pool"][0].rearrange("b t c -> (b t) c")).then_inc(cp_in, 16)
            sp.dma_start(rope_c[:, :], consts[:, c:c + T]).then_inc(rope_in, 16)
            sp.dma_start(rope_s[:, :], consts[:, c + T:c + 2 * T]).then_inc(rope_in, 16)
            sp.dma_start(rcnt[:, :, :], consts[:, c + 2 * T:].rearrange("p (g n) -> p g n", g=4)).then_inc(rope_in, 16)
            sp.dma_start(page_ids[0:1, :], a["page_table"].rearrange("(o b) i -> o (b i)", o=1)).then_inc(ids_in, 16)
            sp.dma_start(o_pools[0, :, 0:NST - 1, :], a["cache_pool"][0, :, 1:NST, :]).then_inc(stored, 16)
            for s in range(2, S_OUT + 3):
                load_w(s)

            kv_pages = a["cache_kv_latent"][0].rearrange("n (p j) r -> n p j r", j=TPP)
            kr_pages = a["cache_k_rope"][0].rearrange("n (p j) r -> n p j r", j=TPP)
            sp.wait_ge(ids_in, 16)
            sp.wait_ge(lo, SPLIT["pm", 3] + 1)
            for keys in (True, False):
                with sp.Fori(0, NB // 2) as it:
                    for u in range(2):
                        sp.wait_ge(c_used[u], it + (1 if keys else 1 + NB // 2))
                        for i in range(NPG):
                            page = sp.value_load(page_ids[0:1, bass.ds(it * 2 * NPG + (u * NPG + i), 1)],
                                                 min_val=0, max_val=NPHYS - 1)
                            rows = slice(16 * i, 16 * i + 16)
                            sp.dma_start(c_ring[rows, u, :, :],
                                         kv_pages[bass.ds(page, 1)].rearrange("o p j r -> (o p) j r")).then_inc(c_in[u], 16)
                            if keys:
                                sp.dma_start(r_ring[rows, u, :, :],
                                             kr_pages[bass.ds(page, 1)].rearrange("o p j r -> (o p) j r")).then_inc(c_in[u], 16)
            sp.wait_ge(lo, SPLIT["uvs",] + 1)
            for t in range(2):
                sp.dma_start(m_nat[:, t, :], a["mem_prompt"][0, t * P:(t + 1) * P, :]).then_inc(mem_in, 16)
            for s in range(S_OUT + 3, S_XO + 2):
                load_w(s)
            full(sp, ("xq", KD - 1, 1))
            for n in range(2 * NB):
                if K3 <= n < NB + K3:
                    freed(sp, ("qb", n - K3, 1))
                elif n >= K3:
                    sp.wait_ge(v_used, n - K3 - NB + 1)
                src = a["cache_mem_k" if n < NB else "cache_mem_v"][0, n % NB]
                sp.dma_start(kv_ring[:, n % K3, :, :], src.rearrange("(p m) h d -> p m (h d)", m=2)).then_inc(kv_in[n % K3], 16)
            for s in range(S_XO + 2, NSLOT):
                load_w(s)
            sp.wait_ge(stored, 16 * 7)
            sp.wait_ge(kv_st, 32)
            sp.wait_ge(y_st[0], 48)
            sp.wait_ge(y_st[1], 32)

        @block.gpsimd
        def _(gp):
            steps, done = [0], [0]

            def step(ins):
                steps[0] += 1
                ins.then_inc(gp_step, 1)
                gp.wait_ge(gp_step, steps[0])

            gp.memset(ones[:, :], 1.0).then_inc(ones_set, 1)
            gp.wait_ge(ones_set, 1)

            def squares(norm, src, chunks, at_):
                prev = {"n1": None, "nq": "n1", "nkv": "nq", "nx": "nkv", "nf": "nx", "nz": "nf"}[norm]
                for c in range(chunks):
                    for f in (0, 1):
                        if norm == "n1":
                            gp.wait_ge(val, VAL["x1", c] + 1 if f == 0 else VAL["xs1",] + 1)
                        else:
                            gp.wait_ge(val, VAL[src, c, f] + 1)
                        if c == 0 and prev:
                            full(gp, ("ssq", prev, f))
                        c0, c1 = HALF[f]
                        x = at_(c)[:, c0:c1]
                        if c == 0:
                            step(gp.tensor_tensor(acc[:, c0:c1], x, x, ALU.mult))
                        else:
                            step(gp.tensor_tensor(sq[:, :], x, x, ALU.mult))
                            ins = gp.tensor_tensor(acc[:, c0:c1], acc[:, c0:c1], sq[:, :], ALU.add)
                            if c == chunks - 1:
                                ins.then_inc(sums, 1)
                                done[0] += 1
                                gp.wait_ge(sums, done[0])
                            else:
                                step(ins)

            squares("n1", "x1", KD, lambda c: xT[:, c, :])
            full(gp, ("in", 0, 0))
            gp.memset(up[:, :, 0:NST], 0.0).then_inc(pads_set, 1)
            gp.wait_ge(pads_set, 1)
            squares("nq", "cq", 3, lambda c: cq[:, c, :])
            squares("nkv", "ckv", 2, lambda c: cT[:, c, :])
            full(gp, ("in", 9, 1))
            for i, t in enumerate((qr_hi, qr_lo)):
                for h in range(NH):
                    r0 = RP * (1 - h % 2)
                    gp.memset(t[r0:r0 + RP, h, :].bitcast(F32), 0.0).then_inc(pads_set, 1)
                    gp.wait_ge(pads_set, NH * i + h + 2)
            for g in range(4):
                gp.wait_ge(val, VAL["up", g, 1] + 1)
                if g:
                    gp.wait_ge(val, VAL["pm", g - 1] + 1)
                src = up[:, g, :]
                n = NST + T
                for lvl in range(g + 1):
                    d = 1 << lvl
                    dst = (ws1, ws2)[(g - lvl) % 2]
                    ins = gp.tensor_tensor(dst[:, 2 * d - 1:n], src[:, 2 * d - 1:n], src[:, d - 1:n - d], ALU.add)
                    if lvl == g:
                        ins.then_inc(winsum, 1)
                        gp.wait_ge(winsum, g + 1)
                    else:
                        step(ins)
                    src = dst
            squares("nx", "xo1", KD, lambda c: xT[:, c, :])
            squares("nf", "xo2", KD, lambda c: xT[:, c, :])
            squares("nz", "xo3", KD, lambda c: xT[:, c, :])

        @block.scalar
        def _(act):
            splits = [0]

            def split_w(s):
                if s >= NSLOT:
                    return
                act.wait_ge(w_loaded[s % RAW], landed[s])
                if s >= SPL:
                    used(act, s - SPL)
                for c0, c1 in pieces(s):
                    act.activation(whi[:, s % SPL, c0:c1], wraw[:, s % RAW, c0:c1], ACT.Copy).then_inc(w_hi, 1)

            def high(key, dst, src, scale=1.0):
                assert SPLIT[key] == splits[0], key
                splits[0] += 1
                act.activation(dst, src, ACT.Copy, scale=scale).then_inc(hi, 1)

            def after(key):
                act.wait_ge(val, VAL[key] + 1)

            def stage(key, dst, src):
                frees(act.activation(dst, src, ACT.Copy), key)

            def roots(norm, t):
                after(("ms", norm) if norm == "mem" else ("ms", norm, 1))
                act.activation(t, t, ACT.Sqrt).then_inc(root, 1)

            split_w(0)
            after(("gT",))
            for c in range(KD):
                after(("x1", c))
                high(("x1", c), B_hi[:, c, 0:TP], xT[:, c, 0:TP], gain(G_MIX + c))
            after(("xs1",))
            for c in range(KD - 1):
                act.activation(B_hi[:, c, TP:T], xT[:, c, TP:T], ACT.Copy, scale=gain(G_MIX + c))
            high(("xs1",), B_hi[:, KD - 1, TP:T], xT[:, KD - 1, TP:T], gain(G_MIX + KD - 1))
            split_w(1)
            for h in range(NH):
                high(("wuk", h), wuk_hi[:, h, :], full(act, ("wuk", h))[:, 0:KVL])
            for m in range(10):
                split_w(S_IN + m + 2)
                if m == 0:
                    roots("n1", rstd[:, :])
                if m == 7:
                    roots("nq", rstd_q[:, :])
                if m == 8:
                    roots("nkv", rstd_kv[:, :])
                if m < 3:
                    for f, (c0, c1) in enumerate(HALF):
                        after(("cq", m, f))
                        high(("cq", m, f), cqg_hi[:, m, c0:c1], cq[:, m, c0:c1], gain(G_Q + m))
                if m == 6:
                    for f, (c0, c1) in enumerate(PROMPT):
                        after(("kr", f))
                        high(("kr", f), kr_hi[:, c0:c1], kr[:, c0:c1])
                if m == 8:
                    for f, (c0, c1) in enumerate(PROMPT):
                        for r in (0, 1):
                            after(("c", r, f))
                            high(("c", r, f), cT_hi[:, r, c0:c1], cT[:, r, c0:c1])
            for h in range(NH):
                if h % 2 == 0:
                    split_w(S_UQ + h // 2 + 2)
                for f, (c0, c1) in enumerate(HALF):
                    after(("qn", h, f))
                    high(("qn", h, f), A_hi[:, h, c0:c1], tmp[:, 2 * (h % 2) + f, :])
            split_w(S_UQ + 4)
            for g in range(4):
                after(("pm", g))
                high(("pm", g), pm_hi[g][:, :], pm[:, :])
            split_w(S_POOL + 2)
            for g in range(4):
                for f, (c0, c1) in enumerate(HALF):
                    high(("py", g, f), A_hi[:, 4 + g, c0:c1], full(act, ("py", g, f))[:, 0:TH], gain(G_PS + g))
                if g < 2:
                    act.wait_ge(pads_set, 9)
                    for f, (c0, c1) in enumerate(HALF):
                        after(("qr", g, f))
                        act.activation(qr_hi[0:RP, 2 * g, c0:c1], qx[0:RP, g, c0:c1], ACT.Copy)
                        high(("qr", g, f), qr_hi[RP:P, 2 * g + 1, c0:c1], qx[RP:P, g, c0:c1])
            for t in range(4):
                stage(("ct", t), c_nat[:, t, :], full(act, ("ct", t))[:, 0:KVL])
            stage(("kt",), kr_nat[:, :, :], full(act, ("kt",))[:, 0:4 * RP].rearrange("p (t r) -> p t r", t=4))
            stage(("smp",), smp_nat[0:NB, :], full(act, ("smp",))[0:NB, 0:KVL + RP])
            stage(("us",), us_nat[0:NB, :], full(act, ("us",))[0:NB, :])
            stage(("ut",), ut_nat[0:NST, :], full(act, ("ut",))[0:NST, :])
            for t in range(4):
                freed(act, ("ct", t))
                high(("cn", t), cn_hi[:, t, :], c_nat[:, t, :])
            act.dma_start(o_kvp[0, 0].rearrange("(t p) r -> p t r", p=P), c_nat[:, :, :]).then_inc(stored, 16)
            freed(act, ("kt",))
            act.dma_start(o_krp[0, 0].rearrange("(t p) r -> p t r", p=P), kr_nat[:, :, :]).then_inc(stored, 16)
            freed(act, ("smp",))
            act.dma_start(o_kvs[0].rearrange("b t r -> (b t) r"), smp_nat[0:NB, 0:KVL]).then_inc(stored, 16)
            act.dma_start(o_krs[0].rearrange("b t r -> (b t) r"), smp_nat[0:NB, KVL:KVL + RP]).then_inc(stored, 16)
            freed(act, ("us",))
            act.dma_start(o_pools[0, :, NST - 1, :], us_nat[0:NB, :]).then_inc(stored, 16)
            freed(act, ("ut",))
            act.dma_start(o_poolp[0, 0], ut_nat[0:NST, :]).then_inc(stored, 16)
            for r in (0, 1):
                high(("ql", 0, r), ql_hi[:, r, :], full(act, ("ql", 0, r)))

            split_w(S_UV + 2)
            us = units()

            def exps(n):
                h, i = us[n]
                b = full(act, ("s", h, i))
                after(("negm", h, i))
                frees(act.activation(prob[:, n % 2, 0:(i + 1) * P], b[:, 0:(i + 1) * P], ACT.Exp,
                                     bias=stat[:, 1, n % 2:n % 2 + 1], scale=MLA_SCALE,
                                     accum_out=stat[:, 2, n % 2:n % 2 + 1]), ("s", h, i))

            exps(0)
            for n, (h, i) in enumerate(us):
                if n + 1 < len(us):
                    exps(n + 1)
                b = full(act, ("pt", h, i))
                high(("pt", h, i), PT_hi[:, 0:i + 1, i * P:(i + 1) * P],
                     b[:, 0:(i + 1) * P].rearrange("p (j q) -> p j q", j=i + 1))
                if i == 0 and h:
                    high(("uv", h - 1), A_hi[:, h - 1, 0:TP], full(act, ("uv", h - 1)))
                if i == 1 and h + 1 < NH:
                    for r in (0, 1):
                        high(("ql", h + 1, r), ql_hi[:, r, :], full(act, ("ql", h + 1, r)))
                if i == 3:
                    for r in (0, 1):
                        high(("pv", h, r), ol_hi[:, r, :], full(act, ("pv", h, r)))
            high(("uv", NH - 1), A_hi[:, NH - 1, 0:TP], full(act, ("uv", NH - 1)))

            for b in range(NB):
                for k in (0, 1):
                    stage(("tb", b, k), cTs[:, b % 2, 0, 4 * k:4 * k + 4, :],
                          full(act, ("tb", b, k)).rearrange("p (j t) -> p j t", j=4))
                stage(("tb", b, 4), rTs[:, b % 2, :, :], full(act, ("tb", b, 4)).rearrange("p (j t) -> p j t", j=4))
            after(("dif",))
            act.activation(Pm[:, :, :, :], Dm[:, :, :, :], ACT.Exp, scale=MLA_SCALE).then_inc(s_exp, 1)
            act.activation(cols[:, 5], cols[:, 4], ACT.Exp, scale=MLA_SCALE).then_inc(s_exp, 1)
            after(("osum",))
            high(("osum",), ols_hi[:, :, :, :], osv[:, :, :, :])
            high(("uvs",), A_hi[:, 0:NH, TP:T], full(act, ("uvs",))[:, 0:NH * NB].rearrange("p (h b) -> p h b", h=NH))

            for m in range(KD):
                split_w(S_OUT + m + 2)
                if m == 1:
                    act.wait_ge(mem_in, 32)
                    for t in (0, 1):
                        act.activation(m_sq[:, t, :], m_nat[:, t, :], ACT.Square, accum_out=mem_ss[:, t:t + 1]).then_inc(mem_sq, 1)
                for f, (c0, c1) in enumerate(HALF):
                    after(("xo1", m, f))
                    high(("xo1", m, f), B_hi[:, m, c0:c1], xT[:, m, c0:c1], gain(G_X + m))
                if m == 1:
                    roots("mem", mem_ss[:, 2:4])
                    for k in range(4):
                        b = full(act, ("mt", k))
                        act.activation(mT_hi[:, 2 * k, :], b[:, 0:NMEM], ACT.Copy, scale=gain(G_MEM + 2 * k))
                        high(("mt", k), mT_hi[:, 2 * k + 1, :], b[:, NMEM:2 * NMEM], gain(G_MEM + 2 * k + 1))

            def rows(n):
                b = full(act, ("mn", n)).rearrange("p (t c) -> p t c", t=2)
                if n == 4:
                    act.wait_ge(kv_st, 16)
                j = n % 4
                stage(("mn", n), kv_nat[:, :, j * 2 * P:(j + 1) * 2 * P], b)
                if n >= 4:
                    freed(act, ("mn", n))
                    high(("mn", n), mvn_hi[:, :, j * 2 * P:(j + 1) * 2 * P], kv_nat[:, :, j * 2 * P:(j + 1) * 2 * P])
                if j == 3:
                    freed(act, ("mn", n))
                    dst = (o_mk, o_mv)[n // 4][0, 0].rearrange("(t p) h d -> p t (h d)", p=P)
                    act.dma_start(dst, kv_nat[:, :, :]).then_inc(kv_st, 16)

            for j in range(16):
                split_w(S_MK + j + 2)
                if 4 <= j < 12:
                    act.wait_ge(lo, SPLIT["mm", j - 4] + 1)
                stage(("mm", j), kv_T[:, j % 4, :], full(act, ("mm", j))[:, 0:NMEM])
                if j < 8:
                    freed(act, ("mm", j))
                    high(("mm", j), mkT_hi[:, j, :], kv_T[:, j % 4, :])
                if j >= 2 and j % 2 == 0:
                    rows(j // 2 - 1)
            rows(7)

            for m in range(KD):
                split_w(S_XQ + m + 2)
                if m == 0:
                    roots("nx", rstd[:, :])
                for f, (c0, c1) in enumerate(PROMPT):
                    after(("xq", m, f))
                    high(("xq", m, f), q_hi[:, m, c0:c1], tmp[:, 2 * (m % 2) + f, 0:c1 - c0])

            def cexps(h):
                after(("cnegm", h))
                for ip in (0, 1):
                    b = full(act, ("cs", h, ip))
                    for i in (0, 1):
                        c = 2 * ip + i
                        ins = act.activation(Pc[:, h % 2, ip, i, :], b[:, i * NMEM:(i + 1) * NMEM], ACT.Exp,
                                             bias=cstat[:, 1, h % 2, c:c + 1], scale=MEM_SCALE,
                                             accum_out=cstat[:, 2, h % 2, c:c + 1])
                    frees(ins, ("cs", h, ip))

            act.wait_ge(kv_st, 32)
            cexps(0)
            for h in range(NH):
                if h + 1 < NH:
                    cexps(h + 1)
                for mb in (0, 1):
                    high(("cpt", h, mb), PTc_hi[:, mb, :], full(act, ("cpt", h, mb)))
                for dc in (0, 1):
                    high(("cpv", h, dc), A_hi[:, 2 * h + dc, 0:TP], full(act, ("cpv", h, dc)))
            after(("cdif",))
            act.activation(Pcs[:, :, :, :], Dc[:, :, :, :], ACT.Exp, scale=MEM_SCALE).then_inc(c_exp, 1)
            act.wait_ge(v_used, NB)
            high(("co",), A_hi[:, :, TP:T], accO[:, 0:KD * NB].rearrange("p (j b) -> p j b", j=KD))

            for m in range(KD):
                split_w(S_XO + m + 2)
                for f, (c0, c1) in enumerate(HALF):
                    after(("xo2", m, f))
                    high(("xo2", m, f), B_hi[:, m, c0:c1], xT[:, m, c0:c1], gain(G_FFN + m))

            for j in range(NF):
                split_w(S_FFN + 2 * j + 2)
                split_w(S_FFN + 2 * j + 3)
                if j == 0:
                    roots("nf", rstd[:, :])
                for f, (c0, c1) in enumerate(HALF):
                    after(("gv", j, f))
                    act.activation(sig[:, f, :], gate[:, f, :], ACT.Sigmoid).then_inc(sig_set, 1)
                for f, (c0, c1) in enumerate(HALF):
                    after(("h", j, f))
                    high(("h", j, f), h_hi[:, j, c0:c1], hv[:, f, :])
            for s in range(S_DOWN + 2, NSLOT):
                split_w(s)
            roots("nz", rstd[:, :])

            for t in range(5):
                n = P if t < 4 else NB
                if t >= 2:
                    act.wait_ge(y_st[t % 2], 16 * (t // 2))
                for k in (0, 1):
                    stage(("y", t, k), y_nat[0:n, t % 2, k * 512:(k + 1) * 512], full(act, ("y", t, k))[0:n, :])
                for k in (0, 1):
                    freed(act, ("y", t, k))
                dst = y_p[0, t * P:(t + 1) * P, :] if t < 4 else y_s.rearrange("b t d -> (b t) d")
                act.dma_start(dst, y_nat[0:n, t % 2, :]).then_inc(y_st[t % 2], 16)
            assert splits[0] == len(SPLIT.at)

        @block.vector
        def _(dve):
            steps, splits, vals = [0], [0], [0]

            def step(ins):
                steps[0] += 1
                ins.then_inc(dve_step, 1)
                dve.wait_ge(dve_step, steps[0])

            def value(key, ins):
                assert VAL[key] == vals[0], key
                vals[0] += 1
                ins.then_inc(val, 1)

            def own(key):
                dve.wait_ge(val, VAL[key] + 1)

            def settle():
                dve.wait_ge(val, vals[0])
                if splits[0]:
                    dve.wait_ge(lo, splits[0])

            def rest(dst, src, high, g=None):
                if g is None:
                    return dve.tensor_tensor(dst, src, high.bitcast(F32), ALU.subtract)
                return dve.scalar_tensor_tensor(dst, src, g, high.bitcast(F32), ALU.mult, ALU.subtract)

            def low(key, dst, src, high, g=None):
                assert SPLIT[key] == splits[0], key
                splits[0] += 1
                dve.wait_ge(hi, SPLIT[key] + 1)
                rest(dst, src, high, g).then_inc(lo, 1)

            def split_w(s):
                if s >= NSLOT:
                    return
                for i, (c0, c1) in enumerate(pieces(s)):
                    dve.wait_ge(w_hi, 2 * s + i + 1)
                    rest(wlo[:, s % SPL, c0:c1], wraw[:, s % RAW, c0:c1], whi[:, s % SPL, c0:c1]).then_inc(w_lo, 1)

            def inverse_rms(norm, width, dst):
                for f, (c0, c1) in enumerate(HALF):
                    b = full(dve, ("ssq", norm, f))
                    value(("ms", norm, f), dve.tensor_scalar(dst[:, c0:c1], b[:, 0:TH], 1.0 / width, EPS, ALU.mult, ALU.add))
                dve.wait_ge(root, ROOTS.index(norm) + 1)
                step(dve.reciprocal(dst[:, :], dst[:, :]))

            def add_residual(key, out_key, m, f):
                c0, c1 = HALF[f]
                b = full(dve, key)
                settle()
                ins = dve.tensor_tensor(xT[:, m, c0:c1], b[:, 0:TH], xT[:, m, c0:c1], ALU.add)
                value(out_key, ins)

            def scaled(key, dst, r, f, out_key):
                c0, c1 = HALF[f]
                b = full(dve, key)
                settle()
                ins = dve.tensor_tensor(dst, b[:, 0:TH], r[:, c0:c1], ALU.mult)
                value(out_key, ins)

            step(dve.memset(qrs[:, :, :, :], 0.0))
            ins = dve.tensor_copy(gT[:, 0:NG], full(dve, ("gain",))[:, 0:NG])
            value(("gT",), ins)
            own(("gT",))
            b = full(dve, ("xs",))
            ins = dve.tensor_copy(xT[:, :, TP:T], b[:, 0:KD * NB].rearrange("p (c n) -> p c n", c=KD))
            value(("xs1",), ins)
            for c in range(KD):
                ins = dve.tensor_copy(xT[:, c, 0:TP], full(dve, ("xt", c)))
                value(("x1", c), ins)
                if c:
                    low(("x1", c - 1), B_lo[:, c - 1, 0:TP], xT[:, c - 1, 0:TP], B_hi[:, c - 1, 0:TP], gain(G_MIX + c - 1))
            low(("x1", KD - 1), B_lo[:, KD - 1, 0:TP], xT[:, KD - 1, 0:TP], B_hi[:, KD - 1, 0:TP], gain(G_MIX + KD - 1))
            dve.wait_ge(hi, SPLIT["xs1",] + 1)
            for c in range(KD - 1):
                rest(B_lo[:, c, TP:T], xT[:, c, TP:T], B_hi[:, c, TP:T], gain(G_MIX + c))
            low(("xs1",), B_lo[:, KD - 1, TP:T], xT[:, KD - 1, TP:T], B_hi[:, KD - 1, TP:T], gain(G_MIX + KD - 1))
            split_w(0)
            split_w(1)
            ins = dve.tensor_copy(cp_T[:, :, :], full(dve, ("cp",))[:, 0:4 * NB * NST].rearrange("p (g n) -> p g n", g=4))
            value(("cpT",), ins)
            for h in range(NH):
                low(("wuk", h), wuk_lo[:, h, :], full(dve, ("wuk", h))[:, 0:KVL], wuk_hi[:, h, :])

            def rope(x, dst, rot_key, f, out_key):
                c0, c1 = HALF[f]
                b = full(dve, rot_key)
                settle()
                dve.tensor_tensor(tmp[:, 0, :], x[:, c0:c1], rope_c[:, c0:c1], ALU.mult)
                frees(dve.tensor_tensor(tmp[:, 1, :], b[:, 0:TH], rope_s[:, c0:c1], ALU.mult), rot_key)
                freed(dve, rot_key)
                value(out_key, dve.tensor_tensor(dst[:, c0:c1], tmp[:, 0, :], tmp[:, 1, :], ALU.add))

            for m in range(10):
                split_w(S_IN + m + 2)
                if m == 0:
                    inverse_rms("n1", D, rstd)
                for f, (c0, c1) in enumerate(HALF):
                    if m < 3:
                        dst, key = cq[:, m, c0:c1], ("cq", m, f)
                    elif m < 5:
                        dst, key = cT[:, m - 3, c0:c1], ("ckv", m - 3, f)
                    elif m == 5:
                        dst, key = krx[:, c0:c1], ("krx", f)
                    else:
                        dst, key = up[:, m - 6, NST + c0:NST + c1], ("up", m - 6, f)
                    scaled(("in", m, f), dst, rstd, f, key)
                if m < 3:
                    for f, (c0, c1) in enumerate(HALF):
                        low(("cq", m, f), cqg_lo[:, m, c0:c1], cq[:, m, c0:c1], cqg_hi[:, m, c0:c1], gain(G_Q + m))
                if m == 6:
                    dve.wait_ge(rope_in, 48)
                    for f, (c0, c1) in enumerate(PROMPT):
                        rope(krx, kr, ("rotk", f), f, ("kr", f))
                    for f, (c0, c1) in enumerate(PROMPT):
                        low(("kr", f), kr_lo[:, c0:c1], kr[:, c0:c1], kr_hi[:, c0:c1])
                if m == 7:
                    inverse_rms("nq", QL, rstd_q)
                if m == 8:
                    inverse_rms("nkv", KVL, rstd_kv)
                    settle()
                    for f, (c0, c1) in enumerate(HALF):
                        for r in (0, 1):
                            value(("c", r, f), dve.scalar_tensor_tensor(cT[:, r, c0:c1], cT[:, r, c0:c1], gain(G_KV + r),
                                                                        rstd_kv[:, c0:c1], ALU.mult, ALU.mult))
                    for f, (c0, c1) in enumerate(PROMPT):
                        for r in (0, 1):
                            low(("c", r, f), cT_lo[:, r, c0:c1], cT[:, r, c0:c1], cT_hi[:, r, c0:c1])
            for h in range(NH):
                if h % 2 == 0:
                    split_w(S_UQ + h // 2 + 2)
                for f in (0, 1):
                    scaled(("un", h, f), tmp[:, 2 * (h % 2) + f, :], rstd_q, f, ("qn", h, f))
                for f, (c0, c1) in enumerate(HALF):
                    low(("qn", h, f), A_lo[:, h, c0:c1], tmp[:, 2 * (h % 2) + f, :], A_hi[:, h, c0:c1])
            split_w(S_UQ + 4)
            for p in (0, 1):
                for f, (c0, c1) in enumerate(HALF):
                    scaled(("ur", p, f), qx[:, p, c0:c1], rstd_q, f, ("qx", p, f))
            for g, win in enumerate(WINDOWS):
                x, ws = up[:, g, NST:NST + T], ws1[:, NST:NST + T]
                dve.wait_ge(winsum, g + 1)
                settle()
                own(("up", g, 1))
                step(dve.scalar_tensor_tensor(pm[:, 0:TP], ws[:, 0:TP], 1.0 / win, x[:, 0:TP], ALU.mult, ALU.subtract))
                c = slice(0, win - 1)
                step(dve.tensor_tensor(ps_[:, 1:3, :].rearrange("p a b -> p (a b)")[:, c], ws[:, c], rcnt[:, g, c], ALU.mult))
                dve.tensor_tensor(pm[:, c], ps_[:, 1:3, :].rearrange("p a b -> p (a b)")[:, c], x[:, c], ALU.subtract)
                old = cp_T[:, g, :].rearrange("p (b t) -> p b t", b=NB)[:, :, NST - win + 1:NST]
                step(dve.tensor_reduce(ps_[:, 0, :], old, AX, ALU.add))
                step(dve.tensor_tensor(ps_[:, 0, :], ps_[:, 0, :], x[:, TP:T], ALU.add))
                value(("pm", g), dve.scalar_tensor_tensor(pm[:, TP:T], ps_[:, 0, :], 1.0 / win, x[:, TP:T], ALU.mult, ALU.subtract))
                low(("pm", g), pm_lo[g][:, :], pm[:, :], pm_hi[g][:, :])
            split_w(S_POOL + 2)
            for g in range(4):
                for f, (c0, c1) in enumerate(HALF):
                    low(("py", g, f), A_lo[:, 4 + g, c0:c1], full(dve, ("py", g, f))[:, 0:TH], A_hi[:, 4 + g, c0:c1],
                        gain(G_PS + g))
                if g < 2:
                    for f in (0, 1):
                        rope(qx[:, g, :], qx[:, g, :], ("rotq", g, f), f, ("qr", g, f))
                    own(("qr", g, 1))
                    for h in (0, 1):
                        for half in (0, 1):
                            dve.tensor_copy(qrs[RP * half:RP * half + RP, :, half, 2 * g + h], qx[RP * h:RP * h + RP, g, TP:T])
                    for f, (c0, c1) in enumerate(HALF):
                        dve.wait_ge(hi, SPLIT["qr", g, f] + 1)
                        rest(qr_lo[0:RP, 2 * g, c0:c1], qx[0:RP, g, c0:c1], qr_hi[0:RP, 2 * g, c0:c1])
                        low(("qr", g, f), qr_lo[RP:P, 2 * g + 1, c0:c1], qx[RP:P, g, c0:c1], qr_hi[RP:P, 2 * g + 1, c0:c1])
            for t in range(4):
                low(("cn", t), cn_lo[:, t, :], c_nat[:, t, :], cn_hi[:, t, :])
            ins = dve.tensor_copy(qls[:, :, :, :], full(dve, ("qls",))[:, 0:2 * NH * NB].rearrange("p (r h b) -> p r h b", r=2, h=NH))
            value(("qls",), ins)
            own(("qls",))
            def over_heads(x):
                return x.unsqueeze(2).to_broadcast([P, NB, NH])
            dve.tensor_tensor(cols[:, 0], qls[:, 0].rearrange("p h b -> p b h"), over_heads(cT[:, 0, TP:T]), ALU.mult)
            dve.tensor_tensor(cols[:, 1], qls[:, 1].rearrange("p h b -> p b h"), over_heads(cT[:, 1, TP:T]), ALU.mult)
            step(dve.tensor_tensor(cols[:, 2], qrs[:, :, 0, :], over_heads(kr[:, TP:T]), ALU.mult))
            step(dve.tensor_tensor(cols[:, 0], cols[:, 0], cols[:, 1], ALU.add))
            value(("sprod",), dve.tensor_tensor(cols[:, 0], cols[:, 0], cols[:, 2], ALU.add))
            for r in (0, 1):
                low(("ql", 0, r), ql_lo[:, r, :], full(dve, ("ql", 0, r)), ql_hi[:, r, :])

            split_w(S_UV + 2)
            us = units()

            def maxes(n):
                h, i = us[n]
                b = full(dve, ("s", h, i))
                settle()
                step(dve.tensor_tensor(b[:, i * P:(i + 1) * P], b[:, i * P:(i + 1) * P], mask[:, :], ALU.add))
                step(dve.reduce_max(stat[:, 0, n % 2:n % 2 + 1], b[:, 0:(i + 1) * P], AX))
                value(("negm", h, i), dve.tensor_scalar(stat[:, 1, n % 2:n % 2 + 1], stat[:, 0, n % 2:n % 2 + 1],
                                                        -MLA_SCALE, None, ALU.mult))

            maxes(0)
            dve.wait_ge(stored, 16 * 7)
            for n, (h, i) in enumerate(us):
                if n + 1 < len(us):
                    maxes(n + 1)
                freed(dve, ("s", h, i))
                step(dve.reciprocal(stat[:, 3, n % 2:n % 2 + 1], stat[:, 2, n % 2:n % 2 + 1]))
                value(("pn", h, i), dve.tensor_scalar(prob[:, n % 2, 0:(i + 1) * P], prob[:, n % 2, 0:(i + 1) * P],
                                                      stat[:, 3, n % 2:n % 2 + 1], None, ALU.mult))
                b = full(dve, ("pt", h, i))
                low(("pt", h, i), PT_lo[:, 0:i + 1, i * P:(i + 1) * P],
                    b[:, 0:(i + 1) * P].rearrange("p (j q) -> p j q", j=i + 1),
                    PT_hi[:, 0:i + 1, i * P:(i + 1) * P])
                if i == 0 and h:
                    low(("uv", h - 1), A_lo[:, h - 1, 0:TP], full(dve, ("uv", h - 1)), A_hi[:, h - 1, 0:TP])
                if i == 1 and h + 1 < NH:
                    for r in (0, 1):
                        low(("ql", h + 1, r), ql_lo[:, r, :], full(dve, ("ql", h + 1, r)), ql_hi[:, r, :])
                if i == 3:
                    for r in (0, 1):
                        low(("pv", h, r), ol_lo[:, r, :], full(dve, ("pv", h, r)), ol_hi[:, r, :])
                if n == 0:
                    frees(dve.tensor_copy(cols[:, 1].rearrange("p b h -> p (b h)"), full(dve, ("snew",))[:, 0:NB * NH]), ("snew",))
            low(("uv", NH - 1), A_lo[:, NH - 1, 0:TP], full(dve, ("uv", NH - 1)), A_hi[:, NH - 1, 0:TP])

            for b in range(NB):
                for k in (2, 3):
                    frees(dve.tensor_copy(cTs[:, b % 2, 1, 4 * (k - 2):4 * (k - 2) + 4, :],
                                          full(dve, ("tb", b, k)).rearrange("p (j t) -> p j t", j=4)), ("tb", b, k))
            for u in (0, 1):
                dve.wait_ge(c_used[u], 1 + NB // 2)

            def column_max(S, n, mxt, mxb, mx_key, diag_key):
                value(mx_key, dve.tensor_reduce(cols[:, 3], S.rearrange("p b j h -> p b h j"), AX, ALU.max))
                b = full(dve, mxt)
                ins = dve.reduce_max(cols[0:NB * NH, 2].rearrange("p b h -> p (b h)")[:, 0:1], b[0:NB * NH, 0:P], AX)
                frees(ins, mxt)
                freed(dve, mxt)
                value(diag_key, dve.tensor_scalar(diag[0:NB * NH, :], ident[0:NB * NH, 0:NB * NH],
                                                  cols[0:NB * NH, 2].rearrange("p b h -> p (b h)")[:, 0:1], None, ALU.mult))
                b = full(dve, mxb)
                frees(dve.tensor_copy(cols[:, 3].rearrange("p b h -> p (b h)"), b[:, 0:NB * NH]), mxb)
                freed(dve, mxb)

            def inner(x, n):
                return x.unsqueeze(2).to_broadcast([P, NB, n, NH])

            S = accS[:, 0:NB * TPP * NH].rearrange("p (b j h) -> p b j h", b=NB, j=TPP)
            freed(dve, ("snew",))
            column_max(S, TPP, ("mxt",), ("mxb",), ("mx",), ("diag",))
            step(dve.tensor_tensor(cols[:, 3], cols[:, 3], cols[:, 1], ALU.max))
            dve.tensor_tensor(cols[:, 4], cols[:, 1], cols[:, 3], ALU.subtract)
            settle()
            value(("dif",), dve.tensor_tensor(Dm[:, :, :, :], S, inner(cols[:, 3], TPP), ALU.subtract))
            dve.wait_ge(s_exp, 2)
            value(("sum",), dve.tensor_reduce(cols[:, 6], Pm[:, :, :, :].rearrange("p b j h -> p b h j"), AX, ALU.add))
            b = full(dve, ("tot",))
            ins = dve.tensor_tensor(cols[:, 7], b[:, 0:NB * NH].rearrange("p (b h) -> p b h", b=NB), cols[:, 5], ALU.add)
            frees(ins, ("tot",))
            freed(dve, ("tot",))
            step(dve.reciprocal(cols[:, 7], cols[:, 7]))
            dve.tensor_tensor(cols[:, 5], cols[:, 5], cols[:, 7], ALU.mult)
            value(("pnorm",), dve.tensor_tensor(Pm[:, :, :, :], Pm[:, :, :, :], inner(cols[:, 7], TPP), ALU.mult))
            own(("pnorm",))
            for r in (0, 1):
                step(dve.tensor_tensor(osv[:, r].rearrange("p h b -> p b h"), cols[:, 5], over_heads(cT[:, r, TP:T]), ALU.mult))
            for u in (0, 1):
                dve.wait_ge(c_used[u], 1 + NB)
            O = accO[:, 0:2 * NB * NH].rearrange("p (r b h) -> p r h b", r=2, b=NB)
            for r in (0, 1):
                ins = dve.tensor_tensor(osv[:, r], O[:, r], osv[:, r], ALU.add)
                if r == 0:
                    step(ins)
            value(("osum",), ins)
            low(("osum",), ols_lo[:, :, :, :], osv[:, :, :, :], ols_hi[:, :, :, :])
            low(("uvs",), A_lo[:, 0:NH, TP:T], full(dve, ("uvs",))[:, 0:NH * NB].rearrange("p (h b) -> p h b", h=NH),
                A_hi[:, 0:NH, TP:T])

            for m in range(KD):
                split_w(S_OUT + m + 2)
                for f in (0, 1):
                    add_residual(("o", m, f), ("xo1", m, f), m, f)
                for f, (c0, c1) in enumerate(HALF):
                    low(("xo1", m, f), B_lo[:, m, c0:c1], xT[:, m, c0:c1], B_hi[:, m, c0:c1], gain(G_X + m))
                if m == 1:
                    dve.wait_ge(mem_sq, 2)
                    value(("ms", "mem"), dve.tensor_scalar(mem_ss[:, 2:4], mem_ss[:, 0:2], 1.0 / D, EPS, ALU.mult, ALU.add))
                    dve.wait_ge(root, ROOTS.index("mem") + 1)
                    step(dve.reciprocal(mem_ss[:, 2:4], mem_ss[:, 2:4]))
                    dve.tensor_scalar(m_nat[:, 0, :], m_nat[:, 0, :], mem_ss[:, 2:3], None, ALU.mult)
                    value(("memn",), dve.tensor_scalar(m_nat[:, 1, :], m_nat[:, 1, :], mem_ss[:, 3:4], None, ALU.mult))
                    for k in range(4):
                        b = full(dve, ("mt", k))
                        dve.wait_ge(hi, SPLIT["mt", k] + 1)
                        rest(mT_lo[:, 2 * k, :], b[:, 0:NMEM], mT_hi[:, 2 * k, :], gain(G_MEM + 2 * k))
                        low(("mt", k), mT_lo[:, 2 * k + 1, :], b[:, NMEM:2 * NMEM], mT_hi[:, 2 * k + 1, :],
                            gain(G_MEM + 2 * k + 1))

            def rows(n):
                if n >= 4:
                    c = slice((n % 4) * 2 * P, (n % 4 + 1) * 2 * P)
                    low(("mn", n), mvn_lo[:, :, c], kv_nat[:, :, c], mvn_hi[:, :, c])

            for j in range(16):
                split_w(S_MK + j + 2)
                if j < 8:
                    low(("mm", j), mkT_lo[:, j, :], kv_T[:, j % 4, :], mkT_hi[:, j, :])
                if j >= 2 and j % 2 == 0:
                    rows(j // 2 - 1)
            rows(7)

            for m in range(KD):
                split_w(S_XQ + m + 2)
                if m == 0:
                    inverse_rms("nx", D, rstd)
                for f in (0, 1):
                    scaled(("xq", m, f), tmp[:, 2 * (m % 2) + f, :], rstd, f, ("xq", m, f))
                own(("xq", m, 1))
                dve.tensor_copy(qcs[:, m, :], tmp[:, 2 * (m % 2) + 1, TH - NB:TH]).then_inc(qcs_set, 1)
                for f, (c0, c1) in enumerate(PROMPT):
                    low(("xq", m, f), q_lo[:, m, c0:c1], tmp[:, 2 * (m % 2) + f, 0:c1 - c0], q_hi[:, m, c0:c1])
            for k in (0, 1):
                frees(dve.tensor_copy(q_nat[0:NB, k * 512:(k + 1) * 512], full(dve, ("qt", k))[0:NB, :]), ("qt", k))

            def cmaxes(h):
                for ip in (0, 1):
                    b = full(dve, ("cs", h, ip)).rearrange("p (i m) -> p i m", i=2)
                    step(dve.reduce_max(cstat[:, 0, h % 2, 2 * ip:2 * ip + 2], b, AX))
                value(("cnegm", h), dve.tensor_scalar(cstat[:, 1, h % 2, :], cstat[:, 0, h % 2, :], -MEM_SCALE, None, ALU.mult))

            def sample_scores(b):
                dve.wait_ge(kv_in[b % K3], 16 * (b // K3 + 1))
                for k in (0, 1):
                    q = full(dve, ("qb", b, k))
                    for h in (2 * k, 2 * k + 1):
                        for m2 in (0, 1):
                            ins = dve.tensor_tensor_reduce(
                                prod[:, :], kv_ring[:, b % K3, m2, h * MD:(h + 1) * MD], q[:, (h % 2) * MD:(h % 2 + 1) * MD],
                                1.0, 0.0, ALU.mult, ALU.add, Sc[:, b, m2, h:h + 1])
                            if (h % 2, m2) != (1, 1):
                                step(ins)
                    frees(ins, ("qb", b, k))
                    freed(dve, ("qb", b, k))

            cmaxes(0)
            for h in range(NH):
                if h + 1 < NH:
                    cmaxes(h + 1)
                for ip in (0, 1):
                    freed(dve, ("cs", h, ip))
                step(dve.reciprocal(cstat[:, 3, h % 2, :], cstat[:, 2, h % 2, :]))
                p4 = Pc[:, h % 2].rearrange("p a b m -> p (a b) m")
                value(("cpn", h), dve.tensor_tensor(p4, p4, cstat[:, 3, h % 2, :].unsqueeze(2).to_broadcast([P, 4, NMEM]), ALU.mult))
                for mb in (0, 1):
                    low(("cpt", h, mb), PTc_lo[:, mb, :], full(dve, ("cpt", h, mb)), PTc_hi[:, mb, :])
                sample_scores(2 * h)
                for dc in (0, 1):
                    low(("cpv", h, dc), A_lo[:, 2 * h + dc, 0:TP], full(dve, ("cpv", h, dc)), A_hi[:, 2 * h + dc, 0:TP])
                sample_scores(2 * h + 1)
            column_max(Sc[:, :, :, :], 2, ("cmxt",), ("cmxb",), ("cmx",), ("cdiag",))
            value(("cdif",), dve.tensor_tensor(Dc[:, :, :, :], Sc[:, :, :, :], inner(cols[:, 3], 2), ALU.subtract))
            dve.wait_ge(c_exp, 1)
            value(("csum",), dve.tensor_reduce(cols[:, 6], Pcs[:, :, :, :].rearrange("p b j h -> p b h j"), AX, ALU.add))
            ins = dve.reciprocal(cols[:, 7].rearrange("p b h -> p (b h)"), full(dve, ("ctot",))[:, 0:NB * NH])
            frees(ins, ("ctot",))
            freed(dve, ("ctot",))
            value(("cpnorm",), dve.tensor_tensor(Pcs[:, :, :, :], Pcs[:, :, :, :], inner(cols[:, 7], 2), ALU.mult))
            low(("co",), A_lo[:, :, TP:T], accO[:, 0:KD * NB].rearrange("p (j b) -> p j b", j=KD), A_hi[:, :, TP:T])

            for m in range(KD):
                split_w(S_XO + m + 2)
                for f in (0, 1):
                    add_residual(("xo", m, f), ("xo2", m, f), m, f)
                for f, (c0, c1) in enumerate(HALF):
                    low(("xo2", m, f), B_lo[:, m, c0:c1], xT[:, m, c0:c1], B_hi[:, m, c0:c1], gain(G_FFN + m))

            for j in range(NF):
                split_w(S_FFN + 2 * j + 2)
                split_w(S_FFN + 2 * j + 3)
                if j == 0:
                    inverse_rms("nf", D, rstd)
                for f in (0, 1):
                    scaled(("g", j, f), gate[:, f, :], rstd, f, ("gv", j, f))
                for f, (c0, c1) in enumerate(HALF):
                    b = full(dve, ("u", j, f))
                    settle()
                    ins = dve.tensor_tensor(upv[:, f, :], b[:, 0:TH], rstd[:, c0:c1], ALU.mult)
                    frees(ins, ("u", j, f))
                    freed(dve, ("u", j, f))
                    step(dve.tensor_tensor(upv[:, f, :], upv[:, f, :], gate[:, f, :], ALU.mult))
                    dve.wait_ge(sig_set, 2 * j + f + 1)
                    value(("h", j, f), dve.tensor_tensor(hv[:, f, :], upv[:, f, :], sig[:, f, :], ALU.mult))
                for f, (c0, c1) in enumerate(HALF):
                    low(("h", j, f), h_lo[:, j, c0:c1], hv[:, f, :], h_hi[:, j, c0:c1])
            for m in range(KD):
                for part in range(3):
                    split_w(S_DOWN + 3 * m + part + 2)
                for f in (0, 1):
                    add_residual(("d", m, f), ("xo3", m, f), m, f)

            inverse_rms("nz", D, rstd)
            for f, (c0, c1) in enumerate(HALF):
                for m in range(KD):
                    value(("yT", m, f), dve.scalar_tensor_tensor(yT[:, m, c0:c1], xT[:, m, c0:c1], gain(G_FIN + m),
                                                                 rstd[:, c0:c1], ALU.mult, ALU.mult))
            assert splits[0] == len(SPLIT.at) and vals[0] == len(VAL.at)

        @block.tensor
        def _(pe):
            uses, order = [0], bank_order()

            def out(key):
                n = BANK[key]
                assert n == uses[0], key
                uses[0] += 1
                if n >= RING:
                    freed(pe, order[n - RING])
                return ps[:, n % RING]

            def filled(ins, key):
                ins.then_inc(bank_full[BANK[key] % RING], 1)

            def after(key):
                pe.wait_ge(val, VAL[key] + 1)

            def split(key):
                pe.wait_ge(lo, SPLIT[key] + 1)

            def weights(s):
                pe.wait_ge(w_lo, 2 * (s + 1))

            def mm3(dst, left, right, first, last):
                pe.matmul(dst, left[0], right[0], start=first, stop=False)
                pe.matmul(dst, left[0], right[1], start=False, stop=False)
                return pe.matmul(dst, left[1], right[0], start=False, stop=last)

            def tile(key, s, rights, c0=0, n=TH, chunks=None):
                b = out(key)
                for k, right in enumerate(rights):
                    ins = mm3(b[:, 0:n], w(s, k, c0), right, k == 0, k == len(rights) - 1)
                filled(ins, key)
                return ins

            def sum_squares(norm, order):
                for f, (c0, c1) in enumerate(HALF):
                    pe.wait_ge(sums, 2 * order + f + 1)
                    key = ("ssq", norm, f)
                    filled(pe.matmul(out(key)[:, 0:TH], ones[:, :], acc[:, c0:c1], start=True, stop=True), key)

            pe.wait_ge(consts_in, 48)
            pe.wait_ge(gains_in, 16 * 8)
            filled(pe.transpose(out(("gain",))[:, 0:NG], gains[0:NG, :], ident[0:NG, 0:NG]), ("gain",))
            pe.wait_ge(x_in, 16 * 5)
            b = out(("xs",))
            for c in range(KD):
                ins = pe.transpose(b[:, c * NB:(c + 1) * NB], x_nat[0:NB, 4, c * P:(c + 1) * P], ident[0:NB, 0:NB])
            filled(ins, ("xs",))
            for c in range(KD):
                b = out(("xt", c))
                for t in range(4):
                    ins = pe.transpose(b[:, t * P:(t + 1) * P], x_nat[:, t, c * P:(c + 1) * P], ident[:, :])
                filled(ins, ("xt", c))
            pe.wait_ge(cp_in, 16)
            b = out(("cp",))
            n = NB * NST
            for g in range(4):
                ins = pe.transpose(b[:, g * n:(g + 1) * n], cp_nat[0:n, g * P:(g + 1) * P], ident[0:n, 0:n])
            filled(ins, ("cp",))
            pe.wait_ge(wuk_in, 16)
            for h in range(NH):
                b = out(("wuk", h))
                for k in (0, 1):
                    ins = pe.transpose(b[:, k * P:(k + 1) * P], wuk_raw[:, k, h * P:(h + 1) * P], ident[:, :])
                filled(ins, ("wuk", h))

            pe.wait_ge(ones_set, 1)
            split(("xs1",))
            for m in range(10):
                weights(S_IN + m)
                for f, (c0, c1) in enumerate(HALF):
                    ins = tile(("in", m, f), S_IN + m, [(B_hi[:, k, c0:c1], B_lo[:, k, c0:c1]) for k in range(KD)])
                if m == 0:
                    sum_squares("n1", 0)
                if m == 6:
                    for f, (c0, c1) in enumerate(HALF):
                        after(("krx", f))
                        filled(pe.matmul(out(("rotk", f))[:, 0:TH], perm[:, :], krx[:, c0:c1], start=True, stop=True), ("rotk", f))
                if m == 7:
                    sum_squares("nq", 1)
                if m == 8:
                    sum_squares("nkv", 2)
            for p, (s, key) in enumerate(((S_UQ, "un"), (S_UQ + 1, "un"), (S_UQ + 2, "ur"))):
                weights(s)
                for i in (0, 1):
                    for f, (c0, c1) in enumerate(HALF):
                        if p == 0 and i == 0:
                            split(("cq", 2, f))
                        ins = tile((key, 2 * p + i if p < 2 else i, f), s,
                                   [(cqg_hi[:, k, c0:c1], cqg_lo[:, k, c0:c1]) for k in range(KQ)], c0=i * P)
            weights(S_POOL)
            for g in range(4):
                split(("pm", g))
                for f, (c0, c1) in enumerate(HALF):
                    key = ("py", g, f)
                    ins = mm3(out(key)[:, 0:TH], w(S_POOL, g), (pm_hi[g][:, c0:c1], pm_lo[g][:, c0:c1]), True, True)
                    filled(ins, key)
                if g < 2:
                    for f, (c0, c1) in enumerate(HALF):
                        after(("qx", g, f))
                        filled(pe.matmul(out(("rotq", g, f))[:, 0:TH], perm[:, :], qx[:, g, c0:c1], start=True, stop=True),
                               ("rotq", g, f))
            for t in range(4):
                b = out(("ct", t))
                for r in (0, 1):
                    ins = pe.transpose(b[:, r * P:(r + 1) * P], cT[:, r, t * P:(t + 1) * P], ident[:, :])
                filled(ins, ("ct", t))
            b = out(("kt",))
            for t in range(4):
                ins = pe.transpose(b[:, t * RP:(t + 1) * RP], kr[0:RP, t * P:(t + 1) * P], ident[0:RP, 0:RP])
            filled(ins, ("kt",))
            b = out(("smp",))
            for r in (0, 1):
                pe.transpose(b[0:NB, r * P:(r + 1) * P], cT[:, r, TP:T], ident[:, :])
            filled(pe.transpose(b[0:NB, KVL:KVL + RP], kr[0:RP, TP:T], ident[0:RP, 0:RP]), ("smp",))
            b = out(("us",))
            for g in range(4):
                ins = pe.transpose(b[0:NB, g * P:(g + 1) * P], up[:, g, NST + TP:NST + T], ident[:, :])
            filled(ins, ("us",))
            b = out(("ut",))
            for g in range(4):
                ins = pe.transpose(b[0:NST, g * P:(g + 1) * P], up[:, g, TP:NST + TP], ident[:, :])
            filled(ins, ("ut",))

            b = out(("qls",))
            for r in (0, 1):
                for h in range(NH):
                    c = (r * NH + h) * NB
                    ins = mm3(b[:, c:c + NB], (wuk_hi[:, h, r * P:(r + 1) * P], wuk_lo[:, h, r * P:(r + 1) * P]),
                              (A_hi[:, h, TP:T], A_lo[:, h, TP:T]), True, True)
                    if r == 0 and h < 2:
                        ins.then_inc(c_used[h], 1)
            filled(ins, ("qls",))

            def latent_queries(h):
                for r in (0, 1):
                    filled(mm3(out(("ql", h, r)), (wuk_hi[:, h, r * P:(r + 1) * P], wuk_lo[:, h, r * P:(r + 1) * P]),
                               (A_hi[:, h, 0:TP], A_lo[:, h, 0:TP]), True, True), ("ql", h, r))

            def scores(h, i):
                q, n = slice(i * P, (i + 1) * P), (i + 1) * P
                b = out(("s", h, i))[:, 0:n]
                split(("ql", h, 1))
                for r in (0, 1):
                    mm3(b, (ql_hi[:, r, q], ql_lo[:, r, q]), (cT_hi[:, r, 0:n], cT_lo[:, r, 0:n]), r == 0, False)
                filled(mm3(b, (qr_hi[:, h, q], qr_lo[:, h, q]), (kr_hi[:, 0:n], kr_lo[:, 0:n]), False, True), ("s", h, i))

            def values(h):
                split(("pt", h, 3))
                for r in (0, 1):
                    b = out(("pv", h, r))
                    for j in range(4):
                        ins = mm3(b[:, j * P:TP], (cn_hi[:, j, r * P:(r + 1) * P], cn_lo[:, j, r * P:(r + 1) * P]),
                                  (PT_hi[:, j, j * P:TP], PT_lo[:, j, j * P:TP]), j == 0, j == 3)
                    filled(ins, ("pv", h, r))

            def up_values(h):
                split(("pv", h, 1))
                b = out(("uv", h))
                for r in (0, 1):
                    ins = mm3(b, w(S_UV, r, h * P), (ol_hi[:, r, :], ol_lo[:, r, :]), r == 0, r == 1)
                filled(ins, ("uv", h))

            us = units()
            latent_queries(0)
            scores(*us[0])
            scores(*us[1])
            after(("sprod",))
            filled(pe.matmul(out(("snew",))[:, 0:NB * NH], ones[:, :], cols[:, 0].rearrange("p b h -> p (b h)"),
                             start=True, stop=True), ("snew",))
            weights(S_UV)
            for n, (h, i) in enumerate(us):
                b = out(("pt", h, i))
                after(("pn", h, i))
                for j in range(i + 1):
                    ins = pe.transpose(b[:, j * P:(j + 1) * P], prob[:, n % 2, j * P:(j + 1) * P], ident[:, :])
                filled(ins, ("pt", h, i))
                if i == 0 and h:
                    up_values(h - 1)
                if n + 2 < len(us):
                    scores(*us[n + 2])
                if i == 1 and h + 1 < NH:
                    latent_queries(h + 1)
                if i == 3:
                    values(h)
            up_values(NH - 1)

            def turn(b):
                u = b % 2
                pe.wait_ge(c_in[u], 16 * 2 * NPG * (b // 2 + 1))
                for k in range(4):
                    r, j0 = k // 2, 4 * (k % 2)
                    dst = out(("tb", b, k))
                    for j in range(4):
                        ins = pe.transpose(dst[:, j * P:(j + 1) * P], c_ring[:, u, j0 + j, r * P:(r + 1) * P], ident[:, :])
                    filled(ins, ("tb", b, k))
                dst = out(("tb", b, 4))
                for j in range(4):
                    ins = pe.transpose(dst[:, j * P:(j + 1) * P],
                                       r_ring[:, u, 2 * j:2 * j + 2, :].rearrange("p a r -> p (a r)"), ident[:, :])
                filled(ins, ("tb", b, 4))

            def past_scores(b):
                u = b % 2
                for k in range(5):
                    freed(pe, ("tb", b, k))
                for j in range(TPP):
                    c = (b * TPP + j) * NH
                    for r in (0, 1):
                        pe.matmul(accS[:, c:c + NH], cTs[:, u, r, j, :], qls[:, r, :, b],
                                  start=(b == 0 and j == 0 and r == 0), stop=False, skip_group_check=True)
                    if j % 2:
                        c -= NH
                        ins = pe.matmul(accS[:, c:c + 2 * NH], rTs[:, u, j // 2, :],
                                        qrs[:, b, :, :].rearrange("p a h -> p (a h)"),
                                        start=False, stop=(b == NB - 1 and j == TPP - 1), skip_group_check=True)
                ins.then_inc(c_used[u], 1)

            turn(0)
            for b in range(NB):
                if b + 1 < NB:
                    turn(b + 1)
                past_scores(b)

            def softmax_sums(mxt, mx, mxb, dg, tot, total):
                b = out(mxt)
                after(mx)
                filled(pe.transpose(b[0:NB * NH, 0:P], cols[:, 3].rearrange("p b h -> p (b h)"), ident[:, :]), mxt)
                b = out(mxb)
                after(dg)
                filled(pe.matmul(b[:, 0:NB * NH], ones[0:NB * NH, :], diag[0:NB * NH, :], start=True, stop=True), mxb)
                b = out(tot)
                after(total)
                filled(pe.matmul(b[:, 0:NB * NH], ones[:, :], cols[:, 6].rearrange("p b h -> p (b h)"), start=True, stop=True), tot)

            softmax_sums(("mxt",), ("mx",), ("mxb",), ("diag",), ("tot",), ("sum",))
            after(("pnorm",))
            for b in range(NB):
                u = b % 2
                pe.wait_ge(c_in[u], 16 * 2 * NPG * (NB // 2) + 16 * NPG * (b // 2 + 1))
                for r in (0, 1):
                    c = (r * NB + b) * NH
                    for j in range(TPP):
                        ins = pe.matmul(accO[:, c:c + NH], c_ring[:, u, j, r * P:(r + 1) * P], Pm[:, b, j, :],
                                        start=(b == 0 and r == 0 and j == 0), stop=(b == NB - 1 and r == 1 and j == TPP - 1),
                                        skip_group_check=True)
                ins.then_inc(c_used[u], 1)
            split(("osum",))
            b = out(("uvs",))
            for h in range(NH):
                for r in (0, 1):
                    ins = mm3(b[:, h * NB:(h + 1) * NB], w(S_UV, r, h * P), (ols_hi[:, r, h, :], ols_lo[:, r, h, :]), r == 0, r == 1)
            filled(ins, ("uvs",))

            split(("uvs",))
            A = lambda c0, c1: [(A_hi[:, k, c0:c1], A_lo[:, k, c0:c1]) for k in range(KD)]
            B = lambda c0, c1: [(B_hi[:, k, c0:c1], B_lo[:, k, c0:c1]) for k in range(KD)]
            for m in range(KD):
                weights(S_OUT + m)
                for f, (c0, c1) in enumerate(HALF):
                    ins = tile(("o", m, f), S_OUT + m, A(c0, c1))
                if m == 1:
                    after(("memn",))
                    for k in range(4):
                        b = out(("mt", k))
                        for c in (0, 1):
                            for t in (0, 1):
                                ins = pe.transpose(b[:, (2 * c + t) * P:(2 * c + t + 1) * P],
                                                   m_nat[:, t, (2 * k + c) * P:(2 * k + c + 1) * P], ident[:, :])
                        filled(ins, ("mt", k))
            def rows(n):
                b = out(("mn", n))
                for i in (0, 1):
                    freed(pe, ("mm", 2 * n + i))
                    for t in (0, 1):
                        ins = pe.transpose(b[:, (2 * t + i) * P:(2 * t + i + 1) * P],
                                           kv_T[:, (2 * n + i) % 4, t * P:(t + 1) * P], ident[:, :])
                filled(ins, ("mn", n))

            for j in range(16):
                weights(S_MK + j)
                tile(("mm", j), S_MK + j, [(mT_hi[:, k, :], mT_lo[:, k, :]) for k in range(KD)], n=NMEM)
                if j >= 2 and j % 2 == 0:
                    rows(j // 2 - 1)
            rows(7)
            for m in range(KD):
                weights(S_XQ + m)
                for f, (c0, c1) in enumerate(HALF):
                    if m == 0:
                        split(("xo1", KD - 1, f))
                    ins = tile(("xq", m, f), S_XQ + m, B(c0, c1))
                if m == 0:
                    sum_squares("nx", 3)
            pe.wait_ge(qcs_set, KD)
            for k in (0, 1):
                b = out(("qt", k))
                for c in range(4):
                    ins = pe.transpose(b[0:NB, c * P:(c + 1) * P], qcs[:, 4 * k + c, :], ident[:, :])
                filled(ins, ("qt", k))

            def mem_scores(h):
                for ip in (0, 1):
                    b = out(("cs", h, ip))
                    for i in (0, 1):
                        q = slice((2 * ip + i) * P, (2 * ip + i + 1) * P)
                        for dc in (0, 1):
                            c = 2 * h + dc
                            ins = mm3(b[:, i * NMEM:(i + 1) * NMEM], (q_hi[:, c, q], q_lo[:, c, q]),
                                      (mkT_hi[:, c, :], mkT_lo[:, c, :]), dc == 0, dc == 1)
                    filled(ins, ("cs", h, ip))

            def spread(b):
                for k in (0, 1):
                    freed(pe, ("qt", k))
                    key = ("qb", b, k)
                    filled(pe.matmul(out(key), ident[0:NB, b:b + 1].to_broadcast([NB, P]), q_nat[0:NB, k * 512:(k + 1) * 512],
                                     start=True, stop=True), key)

            split(("xq", KD - 1, 1))
            split(("mn", 7))
            mem_scores(0)
            for h in range(NH):
                if h + 1 < NH:
                    mem_scores(h + 1)
                after(("cpn", h))
                for mb in (0, 1):
                    b = out(("cpt", h, mb))
                    for i in range(4):
                        ins = pe.transpose(b[:, i * P:(i + 1) * P], Pc[:, h % 2, i // 2, i % 2, mb * P:(mb + 1) * P], ident[:, :])
                    filled(ins, ("cpt", h, mb))
                spread(2 * h)
                split(("cpt", h, 1))
                for dc in (0, 1):
                    b = out(("cpv", h, dc))
                    c = 2 * h + dc
                    for mb in (0, 1):
                        ins = mm3(b, (mvn_hi[:, mb, c * P:(c + 1) * P], mvn_lo[:, mb, c * P:(c + 1) * P]),
                                  (PTc_hi[:, mb, :], PTc_lo[:, mb, :]), mb == 0, mb == 1)
                    filled(ins, ("cpv", h, dc))
                spread(2 * h + 1)
            softmax_sums(("cmxt",), ("cmx",), ("cmxb",), ("cdiag",), ("ctot",), ("csum",))
            after(("cpnorm",))
            for b in range(NB):
                n = NB + b
                pe.wait_ge(kv_in[n % K3], 16 * (n // K3 + 1))
                for c in range(KD):
                    for m2 in (0, 1):
                        ins = pe.matmul(accO[:, c * NB + b:c * NB + b + 1], kv_ring[:, n % K3, m2, c * P:(c + 1) * P],
                                        Pcs[:, b, m2, c // 2:c // 2 + 1], start=(b == 0 and c == 0 and m2 == 0),
                                        stop=(b == NB - 1 and c == KD - 1 and m2 == 1), skip_group_check=True)
                ins.then_inc(v_used, 1)
            split(("co",))
            for m in range(KD):
                weights(S_XO + m)
                for f, (c0, c1) in enumerate(HALF):
                    ins = tile(("xo", m, f), S_XO + m, A(c0, c1))
            for j in range(NF):
                for i, key in enumerate(("g", "u")):
                    s = S_FFN + 2 * j + i
                    weights(s)
                    for f, (c0, c1) in enumerate(HALF):
                        if j == 0 and i == 0:
                            split(("xo2", KD - 1, f))
                        ins = tile((key, j, f), s, B(c0, c1))
                if j == 0:
                    sum_squares("nf", 4)
            for m in range(KD):
                b = [out(("d", m, f)) for f in (0, 1)]
                for part, (k0, k1) in enumerate(DPART):
                    s = S_DOWN + 3 * m + part
                    weights(s)
                    for f, (c0, c1) in enumerate(HALF):
                        if m == 0 and part == 2:
                            split(("h", NF - 1, f))
                        elif m == 0:
                            split(("h", k1 - 1, f))
                        for k in range(k0, k1):
                            ins = mm3(b[f][:, 0:TH], w(s, k - k0), (h_hi[:, k, c0:c1], h_lo[:, k, c0:c1]), k == 0, k == NF - 1)
                        if part == 2:
                            filled(ins, ("d", m, f))
                    if part < 2:
                        ins.then_inc(down_used, 1)
            sum_squares("nz", 5)
            for t in range(5):
                n = P if t < 4 else NB
                c = t * P
                after(("yT", KD - 1, 0 if c + n <= TH else 1))
                for k in (0, 1):
                    b = out(("y", t, k))
                    for i in range(4):
                        ins = pe.transpose(b[0:n, i * P:(i + 1) * P], yT[:, 4 * k + i, c:c + n], ident[:, :])
                    filled(ins, ("y", t, k))
            assert uses[0] == len(BANK.at)


_INS = ["x_prompt", "x_sample", "mem_prompt", "cache_kv_latent", "cache_k_rope", "cache_pool", "cache_mem_k",
        "cache_mem_v", "page_table", "norm_mix", "w_in", "q_norm", "w_uq", "kv_norm", "w_uk", "w_uv", "w_pool",
        "pool_scale", "w_out", "norm_x", "mem_norm", "w_xq", "w_mk", "w_mv", "w_xo", "norm_ffn", "w_gate", "w_up",
        "w_down", "norm_final"]
_OUTS = [(1, TP, D), (NB, 1, D), (1, 1, TP, KVL), (1, 1, TP, RP), (1, 1, NST, PW), (1, 1, NMEM, NH, MD),
         (1, 1, NMEM, NH, MD), (1, NB, 1, KVL), (1, NB, 1, RP), (1, NB, NST, PW)]


def constants():
    f = np.float32
    perm = np.zeros((P, P), f)
    for m in range(P):
        perm[m ^ 32, m] = 1
    q, k = np.meshgrid(np.arange(P), np.arange(P), indexing="ij")
    mask = np.where(k <= q, f(0), f(BIG))
    half = RP // 2
    inv = np.power(f(10000.0), -(np.arange(half, dtype=f) / f(half))).astype(f)
    pos = np.concatenate([np.arange(TP), np.full(NB, PAGE * NPG)]).astype(f)
    ang = (inv[:, None] * pos[None, :]).astype(f)
    cos, sin = np.cos(ang).astype(f), np.sin(ang).astype(f)
    rcnt = np.ones((4, 16), f)
    for g, win in enumerate(WINDOWS):
        rcnt[g] = f(1) / np.minimum(win, np.arange(16) + 1).astype(f)
    rcnt = np.broadcast_to(rcnt.reshape(1, 64), (P, 64))
    return np.ascontiguousarray(np.concatenate(
        [np.eye(P, dtype=f), perm, mask, np.concatenate([cos] * 4), np.concatenate([-sin, sin] * 2), rcnt], 1, dtype=f))


def kernel(**inputs):
    import concourse.bacc as _bacc
    from concourse.bass_utils import run_bass_kernel_spmd as _run

    nc = _bacc.Bacc("TRN2", target_bir_lowering=False, num_devices=1)
    arrays, aps = {}, {}
    for name in _INS:
        x = np.ascontiguousarray(inputs[name])
        arrays[f"in_{name}_dram"] = x
        aps[name] = nc.dram_tensor(f"in_{name}_dram", x.shape, mybir.dt.from_np(x.dtype), kind="ExternalInput").ap()
    table = constants()
    arrays["in_consts_dram"] = table
    consts = nc.dram_tensor("in_consts_dram", table.shape, F32, kind="ExternalInput").ap()
    outs = [nc.dram_tensor(f"out_{i}_dram", shape, F32, kind="ExternalOutput").ap() for i, shape in enumerate(_OUTS)]
    build(nc, aps, consts, outs)
    r = _run(nc, [arrays], core_ids=[0])
    return tuple(r.results[0][f"out_{i}_dram"] for i in range(len(_OUTS)))
```

```python
from contextlib import ExitStack

import numpy as np
import concourse.bass as bass
from concourse import mybir

F32 = mybir.dt.float32
F32R = mybir.dt.float32r
I32 = mybir.dt.int32
U32 = mybir.dt.uint32
ALU = mybir.AluOpType
ACT = mybir.ActivationFunctionType
AX = mybir.AxisListType.X

P = 128
D = 1024
KD = D // P
TP = 512
NB = 8
T = TP + NB
TH = T // 2
HALF = [(0, TH), (TH, T)]
PROMPT = [(0, TH), (TH, TP)]
NH = 4
QL, KVL, RP, PW = 384, 256, 64, 512
NOPE = 128
QH = NOPE + RP
KQ = QL // P
PAGE, NPG = 128, 8
NPHYS = 80
TPP = PAGE * NPG // P
NMEM = 256
MD = 256
FF = 2816
NF = FF // P
WINDOWS = (2, 4, 8, 16)
NST = 15
EPS = 1e-6
MLA_SCALE = float(QH) ** -0.5
MEM_SCALE = float(MD) ** -0.5
BIG = -3.0e38

G_MIX, G_X, G_FFN, G_FIN, G_MEM, G_PS, G_Q, G_KV = 0, 8, 16, 24, 32, 40, 44, 47
NG = 49
NC_CONST = 3 * P + 2 * T + 4 * 16 + 1 + NB
SQ = 32

RAW, SPL = 2, 3
RING = 7

S_IN = 0
S_UQ = S_IN + 10
S_POOL = S_UQ + 3
S_UV = S_POOL + 1
S_OUT = S_UV + 1
S_MK = S_OUT + KD
S_MV = S_MK + KD
S_XQ = S_MV + KD
S_XO = S_XQ + KD
S_FFN = S_XO + KD
S_DOWN = S_FFN + 2 * NF
DPART = [(0, 8), (8, 16), (16, 22)]
NSLOT = S_DOWN + 3 * KD


class Order:

    def __init__(self, keys):
        self.at = {k: n for n, k in enumerate(keys)}
        assert len(self.at) == len(keys)

    def __getitem__(self, key):
        return self.at[key]


def units():
    return [(h, i) for h in range(NH) for i in range(4)]


def bank_order():
    o = [("gain",), ("xs",)] + [("xt", c) for c in range(KD)] + [("cp",)] + [("wuk", h) for h in range(NH)]
    for m in range(10):
        o += [("in", m, f) for f in (0, 1)]
        if m == 0:
            o += [("ssq", "n1", f) for f in (0, 1)]
        if m == 6:
            o += [("rotk", f) for f in (0, 1)]
        if m == 7:
            o += [("ssq", "nq", f) for f in (0, 1)]
        if m == 8:
            o += [("ssq", "nkv", f) for f in (0, 1)]
    o += [("un", h, f) for h in range(NH) for f in (0, 1)]
    o += [("ur", p, f) for p in (0, 1) for f in (0, 1)]
    for g in range(4):
        o += [("py", g, f) for f in (0, 1)]
        if g < 2:
            o += [("rotq", g, f) for f in (0, 1)]
    o += [("ct", t) for t in range(4)] + [("kt",), ("smp",), ("us",), ("ut",), ("qls",)]
    o += [("ql", 0, 0), ("ql", 0, 1), ("s", 0, 0), ("s", 0, 1), ("s", 0, 2), ("snew",)]
    us = units()
    for n, (h, i) in enumerate(us):
        o += [("pt", h, i)]
        if n + 3 < len(us):
            o += [("s",) + us[n + 3]]
        if i == 0 and h + 1 < NH:
            o += [("ql", h + 1, 0), ("ql", h + 1, 1)]
        if i == 0 and h:
            o += [("uv", h - 1)]
        if i == 3:
            o += [("pv", h, 0), ("pv", h, 1)]
    o += [("uv", NH - 1)]
    o += [("own",)] + [("sc", b) for b in range(NB)] + [("ot",), ("uvs",)]
    for m in range(KD):
        o += [("o", m, f) for f in (0, 1)]
        if m == 1:
            o += [("mt", k) for k in range(4)]
    for j in range(16):
        o += [("mm", j)]
        if j >= 2 and j % 2 == 0:
            o += [("mn", j // 2 - 1)]
    o += [("mn", 7)]
    for m in range(KD):
        o += [("xq", m, f) for f in (0, 1)]
        if m == 0:
            o += [("ssq", "nx", f) for f in (0, 1)]
    o += [("qt", 0), ("qt", 1), ("cs", 0, 0), ("cs", 0, 1)]
    for h in range(NH):
        if h + 1 < NH:
            o += [("cs", h + 1, 0), ("cs", h + 1, 1)]
        o += [("cpt", h, 0), ("cpt", h, 1), ("qb", 2 * h, 0), ("qb", 2 * h, 1)]
        o += [("cpv", h, 0), ("cpv", h, 1), ("qb", 2 * h + 1, 0), ("qb", 2 * h + 1, 1)]
    o += [("cmxt",), ("cmxb",), ("ctot",)]
    o += [("xo", m, f) for m in range(KD) for f in (0, 1)]
    for j in range(NF):
        o += [("g", j, 0), ("g", j, 1), ("u", j, 0), ("u", j, 1)]
        if j == 0:
            o += [("ssq", "nf", f) for f in (0, 1)]
    o += [("d", m, f) for m in range(KD) for f in (0, 1)]
    o += [("ssq", "nz", f) for f in (0, 1)]
    o += [("y", t, k) for t in range(5) for k in (0, 1)]
    return o


def val_order():
    o = [("gT",), ("xs1",)] + [("x1", c) for c in range(KD)] + [("cpT",)]
    for m in range(10):
        if m == 0:
            o += [("ms", "n1", f) for f in (0, 1)]
        if m < 3:
            o += [("cq", m, f) for f in (0, 1)]
        elif m < 5:
            o += [("ckv", m - 3, f) for f in (0, 1)]
        elif m == 5:
            o += [("krx", f) for f in (0, 1)]
        else:
            o += [("up", m - 6, f) for f in (0, 1)]
        if m == 6:
            o += [("kr", f) for f in (0, 1)]
        if m == 7:
            o += [("ms", "nq", f) for f in (0, 1)]
        if m == 8:
            o += [("ms", "nkv", f) for f in (0, 1)]
            o += [("c", r, f) for f in (0, 1) for r in (0, 1)]
    o += [("qn", h, f) for h in range(NH) for f in (0, 1)]
    o += [("qx", p, f) for p in (0, 1) for f in (0, 1)]
    o += [("pm", g) for g in range(4)]
    o += [("qr", p, f) for p in (0, 1) for f in (0, 1)]
    o += [("qls",), ("sprod",)]
    us = units()
    o += [("negm",) + us[0], ("negm",) + us[1], ("pn",) + us[0]]
    for n in range(len(us)):
        o += [("pn",) + v for v in us[n + 1:n + 2]] + [("negm",) + v for v in us[n + 2:n + 3]]
    o += [("turned", b) for b in range(NB)] + [("bias",), ("own_p",), ("spread_p",), ("rows",)]
    for m in range(KD):
        o += [("xo1", m, f) for f in (0, 1)]
        if m == 1:
            o += [("ms", "mem"), ("memn",)]
    o += [("ms", "nx", f) for f in (0, 1)]
    for m in range(KD):
        o += [("xq", m, f) for f in (0, 1)]
    o += [("cnegm", 0)]
    for h in range(NH):
        o += [("cnegm", v) for v in range(h + 1, min(h + 2, NH))] + [("cpn", h)]
    o += [("cmx",), ("cdiag",), ("cdif",), ("csum",), ("cpnorm",)]
    o += [("xo2", m, f) for m in range(KD) for f in (0, 1)]
    o += [("ms", "nf", f) for f in (0, 1)]
    for j in range(NF):
        o += [("gv", j, 0), ("gv", j, 1), ("h", j, 0), ("h", j, 1)]
    o += [("xo3", m, f) for m in range(KD) for f in (0, 1)]
    o += [("ms", "nz", f) for f in (0, 1)]
    o += [("yT", m, f) for f in (0, 1) for m in range(KD)]
    return o


def split_order():
    o = [("x1", c) for c in range(KD)] + [("xs1",)] + [("wuk", h) for h in range(NH)]
    for m in range(10):
        if m < 3:
            o += [("cq", m, f) for f in (0, 1)]
        if m == 6:
            o += [("kr", f) for f in (0, 1)]
        if m == 8:
            o += [("c", r, f) for f in (0, 1) for r in (0, 1)]
    o += [("qn", h, f) for h in range(NH) for f in (0, 1)]
    for g in range(4):
        o += [("pm", g)]
    for g in range(4):
        o += [("py", g, f) for f in (0, 1)]
        if g < 2:
            o += [("qr", g, f) for f in (0, 1)]
    o += [("cn", t) for t in range(4)]
    o += [("ql", 0, 0), ("ql", 0, 1)]
    for h, i in units():
        o += [("pt", h, i)]
        if i == 0 and h + 1 < NH:
            o += [("ql", h + 1, 0), ("ql", h + 1, 1)]
        if i == 0 and h:
            o += [("uv", h - 1)]
        if i == 3:
            o += [("pv", h, 0), ("pv", h, 1)]
    o += [("uv", NH - 1), ("ot",), ("uvs",)]
    for m in range(KD):
        o += [("xo1", m, f) for f in (0, 1)]
        if m == 1:
            o += [("mt", k) for k in range(4)]
    for j in range(16):
        if j < 8:
            o += [("mm", j)]
        if j >= 2 and j % 2 == 0 and j // 2 - 1 >= 4:
            o += [("mn", j // 2 - 1)]
    o += [("mn", 7)]
    o += [("xq", m, f) for m in range(KD) for f in (0, 1)]
    for h in range(NH):
        o += [("cpt", h, 0), ("cpt", h, 1), ("cpv", h, 0), ("cpv", h, 1)]
    o += [("co",)]
    o += [("xo2", m, f) for m in range(KD) for f in (0, 1)]
    o += [("h", j, f) for j in range(NF) for f in (0, 1)]
    return o


ROOTS = ["n1", "nq", "nkv", "mem", "nx", "nf", "nz"]


def in_value(m, f):
    if m < 3:
        return ("cq", m, f)
    if m < 5:
        return ("ckv", m - 3, f)
    return ("krx", f) if m == 5 else ("up", m - 6, f)


BY_LOW = ("ot", "wuk", "py", "ql", "pt", "uv", "pv", "uvs", "mt", "cpt", "cpv")
BY_VALUE = {
    "ssq": lambda norm, f: ("ms", norm, f),
    "gain": lambda: ("gT",), "xs": lambda: ("xs1",), "xt": lambda c: ("x1", c), "cp": lambda: ("cpT",),
    "in": in_value, "un": lambda h, f: ("qn", h, f), "ur": lambda p, f: ("qx", p, f), "qls": lambda: ("qls",),
    "o": lambda m, f: ("xo1", m, f), "xq": lambda m, f: ("xq", m, f), "xo": lambda m, f: ("xo2", m, f),
    "g": lambda j, f: ("gv", j, f), "d": lambda m, f: ("xo3", m, f),
}


def build(nc, a, consts, outs):
    (y_p, y_s, o_kvp, o_krp, o_poolp, o_mk, o_mv, o_kvs, o_krs, o_pools) = outs
    BANK, VAL, SPLIT = Order(bank_order()), Order(val_order()), Order(split_order())
    ctx = ExitStack()
    with ctx:
        base = -(-nc.sbuf_base // 64) * 64
        RB = T * 4
        where = {"at": base}

        def take(n):
            at = where["at"]
            where["at"] = at + -(-n // 32) * 32
            assert where["at"] <= nc.sbuf_usable_end, where["at"]
            return at

        def at(name, shape, dt, offset):
            return nc.alloc_sbuf_tensor_at(name, [P] + shape, dt, offset=offset)

        def keep(name, shape, dt=F32):
            return at(name, shape, dt, take(4 * int(np.prod(shape))))

        xT = keep("xT", [KD, T])
        wraw = keep("wraw", [RAW, 1024])
        whi = keep("whi", [SPL, 1024], F32R)
        wlo = keep("wlo", [SPL, 1024], F32R)
        ident = keep("ident", [P])
        perm = keep("perm", [P])
        mask = keep("mask", [P])
        small = keep("small", [4 * 16 + 1 + NB])
        rcnt = small[:, 0:4 * 16].rearrange("p (g n) -> p g n", g=4)
        row_in_page = small[:, 4 * 16:4 * 16 + 1]
        is_sample = small[:, 4 * 16 + 1:]
        ones = keep("ones", [P])
        gT = keep("gT", [64])
        rstd = keep("rstd", [T])
        rstd_q = keep("rstd_q", [T])
        acc = keep("acc", [T])
        sq = keep("sq", [TH])
        o_tmp = where["at"]
        tmp = keep("tmp", [4, TH])
        qls = keep("qls", [2, NH, NB])
        stat = keep("stat", [4, 4])
        cstat = keep("cstat", [4, 2, 4])
        mem_ss = keep("mem_ss", [4])
        cols = keep("cols", [8, NB, NH])
        diag = keep("diag", [NB * NH])
        ps_ = keep("ps_", [4, NB])
        page_ids = keep("page_ids", [NB], I32)
        row_ids = keep("row_ids", [NB], U32)
        own_c = keep("own_c", [2, NB, NH])
        srow = keep("srow", [16])

        b0 = take(16 * RB)
        B_hi = at("B_hi", [KD, T], F32R, b0)
        B_lo = at("B_lo", [KD, T], F32R, b0 + KD * RB)
        a0 = take(16 * RB)
        A_hi = at("A_hi", [KD, T], F32R, a0)
        A_lo = at("A_lo", [KD, T], F32R, a0 + KD * RB)
        g0 = where["at"]
        g1 = nc.sbuf_usable_end

        where["at"] = g0
        rope_c = keep("rope_c", [T])
        rope_s = keep("rope_s", [T])
        cT = keep("cT", [2, T])
        kr = keep("kr", [T])
        o_keys = where["at"]
        cT_hi = keep("cT_hi", [2, TP], F32R)
        cT_lo = keep("cT_lo", [2, TP], F32R)
        kr_hi = keep("kr_hi", [TP], F32R)
        kr_lo = keep("kr_lo", [TP], F32R)
        o_cn = where["at"]
        cn_hi = keep("cn_hi", [4, KVL], F32R)
        cn_lo = keep("cn_lo", [4, KVL], F32R)
        o_wuk = where["at"]
        wuk_hi = keep("wuk_hi", [NH, KVL], F32R)
        wuk_lo = keep("wuk_lo", [NH, KVL], F32R)
        cp_T = at("cp_T", [4, NB * NST], F32, a0 + 4 * RB)
        o_cq = take(6 * RB)
        cqg_hi = at("cqg_hi", [3, T], F32R, o_cq)
        cqg_lo = at("cqg_lo", [3, T], F32R, o_cq + 3 * RB)
        PT_hi = at("PT_hi", [4, TP], F32R, o_cq)
        prob = [at(f"prob{i}", [(i + 1) * P], F32, o) for i, o in
                enumerate((o_tmp, o_tmp + P * 4, o_cq + 4 * TP * 4, o_cq + 4 * TP * 4 + 3 * P * 4))]
        o_ring = take(20480)
        x_nat = at("x_nat", [5, D], F32, o_ring)
        up = at("up", [4, NST + T], F32, o_ring)
        ws1 = at("ws1", [NST + T], F32, o_ring + 8576)
        ws2 = at("ws2", [NST + T], F32, o_ring + 10720)
        pm = at("pm", [T], F32, o_ring + 12864)
        o_ol = take(4 * RB)
        ol_hi = at("ol_hi", [2, TP], F32R, o_ol)
        ol_lo = at("ol_lo", [2, TP], F32R, o_ol + 2 * TP * 4)
        cq = at("cq", [3, T], F32, o_ol)
        qx = at("qx", [2, T], F32, o_ol)
        rstd_kv = at("rstd_kv", [T], F32, o_ol + 2 * RB)
        krx = at("krx", [T], F32, o_ol + 3 * RB)
        o_b1, o_b2, o_b3 = b0, b0 + 4 * RB, b0 + 12 * RB
        ql_hi = at("ql_hi", [2, TP], F32R, o_b1)
        ql_lo = at("ql_lo", [2, TP], F32R, o_b1 + 2 * TP * 4)
        pm_hi = [at(f"pm_hi{g}", [T], F32R, (o_b1, o_b1, o_b3, o_b3)[g] + 2 * (g % 2) * RB) for g in range(4)]
        pm_lo = [at(f"pm_lo{g}", [T], F32R, (o_b1, o_b1, o_b3, o_b3)[g] + (2 * (g % 2) + 1) * RB) for g in range(4)]
        qr_hi = at("qr_hi", [NH, T], F32R, o_b2)
        qr_lo = at("qr_lo", [NH, T], F32R, o_b2 + 4 * RB)
        PT_lo = at("PT_lo", [4, TP], F32R, o_b3)
        wuk_raw = at("wuk_raw", [2, NH * NOPE], F32, a0)
        gains = at("gains", [P], F32, a0 + 4096)
        cp_nat = at("cp_nat", [PW], F32, a0 + 4096 + 512)
        c_nat = at("c_nat", [4, KVL], F32, o_b3)
        kr_nat = at("kr_nat", [4, RP], F32, o_b3 + 4096)
        smp_nat = at("smp_nat", [KVL + RP], F32, o_b3 + 5120)
        us_nat = at("us_nat", [PW], F32, g0)
        ut_nat = at("ut_nat", [PW], F32, g0 + RB)
        CB, RPB = TPP * KVL * 4, TPP * RP * 4
        c_at = [o_ring, o_ring + CB, g0, o_keys, o_b3, o_cn, o_cq, o_ol]
        r_at = [o_ring + 2 * CB, o_ring + 2 * CB + RPB, g0 + CB, o_keys + CB, o_keys + CB + RPB, o_cq + CB,
                o_cq + CB + RPB, o_ring + 2 * CB]
        past_c = [at(f"past_c{b}", [TPP, KVL], F32, c_at[b]) for b in range(NB)]
        past_r = [at(f"past_r{b}", [TPP, RP], F32, r_at[b]) for b in range(NB)]
        turned_c = at("turned_c", [2, TPP, KVL // SQ, SQ], F32, b0)
        turned_r = at("turned_r", [2, TPP, RP // SQ, SQ], F32, b0 + 2 * CB)
        o_s = b0 + 2 * (CB + RPB)
        NK = (KVL + RP) // SQ
        q_diag = at("q_diag", [NK, P // SQ, NB, NH], F32, o_wuk)
        S = at("S", [TPP, SQ], F32, o_s)
        own_nat = at("own_nat", [KVL], F32, o_s + 1024)
        PT = at("PT", [TPP, NB, NH], F32, o_s + 2048)
        o_rows = at("o_rows", [KVL], F32, o_wuk + NK * P * 4)
        PS = TPP * SQ + NH
        P_pad = at("P_pad", [NB * PS], F32, b0)
        ols_hi = at("ols_hi", [2, NH, NB], F32R, o_s + 3072)
        ols_lo = at("ols_lo", [2, NH, NB], F32R, o_s + 3328)
        qrs = at("qrs", [NB, NH], F32, take(128))
        where["at"] = g0
        q_hi = keep("q_hi", [KD, TP], F32R)
        q_lo = keep("q_lo", [KD, TP], F32R)
        mT_hi = at("mT_hi", [KD, NMEM], F32R, g0)
        mT_lo = at("mT_lo", [KD, NMEM], F32R, g0 + KD * NMEM * 4)
        m_nat = at("m_nat", [2, D], F32, g0 + 2 * KD * NMEM * 4)
        mkT_hi = keep("mkT_hi", [KD, NMEM], F32R)
        mkT_lo = keep("mkT_lo", [KD, NMEM], F32R)
        mvn_hi = keep("mvn_hi", [2, D], F32R)
        mvn_lo = keep("mvn_lo", [2, D], F32R)
        o_pc = take(14080)
        PTc_hi = at("PTc_hi", [2, TP], F32R, o_pc)
        PTc_lo = at("PTc_lo", [2, TP], F32R, o_pc + 4096)
        kv_nat = at("kv_nat", [2, D], F32, o_pc)
        m_sq = at("m_sq", [2, D], F32, o_pc)
        kv_T = at("kv_T", [4, NMEM], F32, o_pc + 8192)
        q_nat = at("q_nat", [D], F32, o_pc + 8192)
        prod = at("prod", [MD], F32, o_pc + 12288)
        Sc = at("Sc", [NB, 2, NH], F32, o_pc + 13312)
        Dc = at("Dc", [NB, 2, NH], F32, o_pc + 13568)
        Pcs = at("Pcs", [NB, 2, NH], F32, o_pc + 13824)
        K3 = 3
        kv_ring = at("kv_ring", [K3, 2, D], F32, b0)
        Pc = at("Pc", [2, 2, 2, NMEM], F32, b0 + K3 * 8192)
        qcs = at("qcs", [KD, NB], F32, take(256))
        where["at"] = a0
        h_hi = keep("h_hi", [NF, T], F32R)
        h_lo = keep("h_lo", [NF, T], F32R)
        gate = keep("gate", [2, TH])
        sig = keep("sig", [2, TH])
        upv = keep("upv", [2, TH])
        hv = keep("hv", [2, TH])
        yT = at("yT", [KD, T], F32, b0)
        y_nat = at("y_nat", [2, D], F32, b0 + KD * RB)

        ps = ctx.enter_context(nc.psum_tensor("ps", [P, 8, 512], F32))
        accO = ps[:, RING]

        def sem(name):
            return ctx.enter_context(nc.semaphore(name))

        bank_full = [sem(f"bank_full{i}") for i in range(RING)]
        bank_free = [sem(f"bank_free{i}") for i in range(RING)]
        w_loaded = [sem(f"w_loaded{i}") for i in range(RAW)]
        w_hi, w_lo = sem("w_hi"), sem("w_lo")
        down_used = sem("down_used")
        val = sem("val")
        hi, lo = sem("hi"), sem("lo")
        root = sem("root")
        sums = sem("sums")
        dve_step, act_step, gp_step = sem("dve_step"), sem("act_step"), sem("gp_step")
        consts_in, gains_in, x_in, wuk_in, cp_in, rope_in, ids_in, mem_in = (
            sem(n) for n in ("consts_in", "gains_in", "x_in", "wuk_in", "cp_in", "rope_in", "ids_in", "mem_in"))
        ones_set, pads_set = sem("ones_set"), sem("pads_set")
        winsum = sem("winsum")
        rows_known = sem("rows_known")
        c_in = [sem(f"c_in{b}") for b in range(NB)]
        own_set = sem("own_set")
        q_zero = sem("q_zero")
        q_built = sem("q_built")
        pad_set = sem("pad_set")
        past_mixed = sem("past_mixed")
        kv_in = [sem(f"kv_in{i}") for i in range(K3)]
        v_used = sem("v_used")
        mem_sq = sem("mem_sq")
        s_exp, c_exp = sem("s_exp"), sem("c_exp")
        sig_set = sem("sig_set")
        qcs_set = sem("qcs_set")
        stored = sem("stored")
        kv_st = sem("kv_st")
        y_st = [sem(f"y_st{i}") for i in range(2)]

        def gain(row):
            return gT[:, row:row + 1]

        def full(eng, key):
            n = BANK[key]
            eng.wait_ge(bank_full[n % RING], n // RING + 1)
            return ps[:, n % RING]

        own_frees = [0] * RING
        free_count = {}
        for n, key in enumerate(bank_order()):
            if key[0] not in BY_LOW and key[0] not in BY_VALUE:
                own_frees[n % RING] += 1
                free_count[key] = own_frees[n % RING]

        def freed(eng, key):
            if key[0] in BY_LOW:
                eng.wait_ge(lo, SPLIT[key] + 1)
            elif key[0] in BY_VALUE:
                eng.wait_ge(val, VAL[BY_VALUE[key[0]](*key[1:])] + 1)
            else:
                eng.wait_ge(bank_free[BANK[key] % RING], free_count[key])

        def frees(ins, key):
            assert key in free_count
            ins.then_inc(bank_free[BANK[key] % RING], 1)

        w_in, w_uq, w_uv = a["w_in"][0], a["w_uq"][0], a["w_uv"][0]

        def columns(w, c0, k0=0, k1=KD, n=P):
            return w[k0 * P:k1 * P, c0:c0 + n].rearrange("(k p) n -> p k n", p=P)

        slots = []

        def slot(k, n, parts):
            slots.append((k, n, parts))

        in_cols = [0, 128, 256, 384, 512, None, 704, 832, 960, 1088]
        for c0 in in_cols:
            if c0 is None:
                r0 = QL + KVL
                slot(KD, P, [(0, RP, columns(w_in, r0, n=RP)), (RP, RP, columns(w_in, r0, n=RP))])
            else:
                slot(KD, P, [(0, P, columns(w_in, c0))])
        for h0 in (0, 2):
            slot(KQ, 2 * P, [(P * i, P, columns(w_uq, (h0 + i) * QH, 0, KQ)) for i in (0, 1)])
        slot(KQ, 2 * P, [(RP * i, RP, columns(w_uq, i * QH + NOPE, 0, KQ, RP)) for i in range(NH)])
        slot(4, P, [(0, P, a["w_pool"][0].rearrange("g c d -> c g d"))])
        slot(2, PW, [(0, PW, w_uv.rearrange("(k p) h v -> p k (h v)", p=P))])
        for name in ("w_out", "w_mk", "w_mv", "w_xq", "w_xo"):
            for m in range(KD):
                slot(KD, P, [(0, P, columns(a[name][0], m * P))])
        for j in range(NF):
            for name in ("w_gate", "w_up"):
                slot(KD, P, [(0, P, columns(a[name][0], j * P))])
        for m in range(KD):
            for k0, k1 in DPART:
                slot(k1 - k0, P, [(0, P, columns(a["w_down"][0], m * P, k0, k1))])
        assert len(slots) == NSLOT
        landed, count = [], [0] * RAW
        for s, (_, _, parts) in enumerate(slots):
            count[s % RAW] += 16 * len(parts)
            landed.append(count[s % RAW])

        def used(eng, s):
            if s >= S_DOWN:
                m, part = divmod(s - S_DOWN, 3)
                if part == 2:
                    full(eng, ("d", m, 1))
                else:
                    eng.wait_ge(down_used, 2 * m + part + 1)
            elif s >= S_FFN:
                j, i = divmod(s - S_FFN, 2)
                full(eng, ("gu"[i], j, 1))
            elif s >= S_XO:
                full(eng, ("xo", s - S_XO, 1))
            elif s >= S_XQ:
                full(eng, ("xq", s - S_XQ, 1))
            elif s >= S_MK:
                full(eng, ("mm", s - S_MK))
            elif s >= S_OUT:
                full(eng, ("o", s - S_OUT, 1))
            elif s >= S_UQ:
                full(eng, {S_UQ: ("un", 1, 1), S_UQ + 1: ("un", 3, 1), S_UQ + 2: ("ur", 1, 1),
                           S_POOL: ("py", 3, 1), S_UV: ("uvs",)}[s])
            else:
                full(eng, ("in", s - S_IN, 1))

        def pieces(s):
            n = slots[s][0] * slots[s][1]
            return [(0, n // 2), (n // 2, n)]

        def w(s, k, c0=0, n=P):
            o = k * slots[s][1] + c0
            return whi[:, s % SPL, o:o + n], wlo[:, s % SPL, o:o + n]

        block = ctx.enter_context(nc.Block())

        @block.sync
        def _(sp):
            def load_w(s):
                if s >= RAW:
                    sp.wait_ge(w_lo, 2 * (s - RAW + 1))
                k, n, parts = slots[s]
                view = wraw[:, s % RAW, 0:k * n].rearrange("p (k n) -> p k n", k=k)
                for c0, width, src in parts:
                    sp.dma_start(view[:, :, c0:c0 + width], src).then_inc(w_loaded[s % RAW], 16)

            c = 0
            for t, n in ((ident, P), (perm, P), (mask, P)):
                sp.dma_start(t[:, :], consts[:, c:c + n]).then_inc(consts_in, 16)
                c += n
            row = 0
            for name, n in (("norm_mix", 8), ("norm_x", 8), ("norm_ffn", 8), ("norm_final", 8), ("mem_norm", 8),
                            ("pool_scale", 4), ("q_norm", 3), ("kv_norm", 2)):
                g = a[name] if name == "norm_final" else a[name][0]
                sp.dma_start(gains[row:row + n, :], g.rearrange("(c p) -> c p", p=P)).then_inc(gains_in, 16)
                row += n
            sp.dma_start(x_nat[0:NB, 4, :], a["x_sample"].rearrange("b t d -> (b t) d")).then_inc(x_in, 16)
            for t in range(4):
                sp.dma_start(x_nat[:, t, :], a["x_prompt"][0, t * P:(t + 1) * P, :]).then_inc(x_in, 16)
            load_w(0)
            load_w(1)
            sp.dma_start(wuk_raw[:, :, :], a["w_uk"][0].rearrange("(k p) h n -> p k (h n)", p=P)).then_inc(wuk_in, 16)
            sp.dma_start(cp_nat[0:NB * NST, :], a["cache_pool"][0].rearrange("b t c -> (b t) c")).then_inc(cp_in, 16)
            sp.dma_start(rope_c[:, :], consts[:, c:c + T]).then_inc(rope_in, 16)
            sp.dma_start(rope_s[:, :], consts[:, c + T:c + 2 * T]).then_inc(rope_in, 16)
            sp.dma_start(small[:, :], consts[:, c + 2 * T:]).then_inc(rope_in, 16)
            for i in range(NPG):
                rows = slice(i * P // NPG, (i + 1) * P // NPG)
                sp.dma_start(page_ids[rows, :], a["page_table"][:, i:i + 1].rearrange("b o -> o b")
                             .to_broadcast([P // NPG, NB]), allow_slow_non_contiguous=True).then_inc(ids_in, 16)
            sp.dma_start(o_pools[0, :, 0:NST - 1, :], a["cache_pool"][0, :, 1:NST, :]).then_inc(stored, 16)
            for s in range(2, S_OUT + 3):
                load_w(s)

            sp.wait_ge(lo, SPLIT["uvs",] + 1)
            for t in range(2):
                sp.dma_start(m_nat[:, t, :], a["mem_prompt"][0, t * P:(t + 1) * P, :]).then_inc(mem_in, 16)
            for s in range(S_OUT + 3, S_XO + 2):
                load_w(s)
            full(sp, ("xq", KD - 1, 1))
            for n in range(2 * NB):
                if K3 <= n < NB + K3:
                    freed(sp, ("qb", n - K3, 1))
                elif n >= K3:
                    sp.wait_ge(v_used, n - K3 - NB + 1)
                src = a["cache_mem_k" if n < NB else "cache_mem_v"][0, n % NB]
                sp.dma_start(kv_ring[:, n % K3, :, :], src.rearrange("(p m) h d -> p m (h d)", m=2)).then_inc(kv_in[n % K3], 16)
            for s in range(S_XO + 2, NSLOT):
                load_w(s)
            sp.wait_ge(stored, 16 * 7)
            sp.wait_ge(kv_st, 32)
            sp.wait_ge(y_st[0], 48)
            sp.wait_ge(y_st[1], 32)

        @block.gpsimd
        def _(gp):
            steps, done = [0], [0]

            def step(ins):
                steps[0] += 1
                ins.then_inc(gp_step, 1)
                gp.wait_ge(gp_step, steps[0])

            gp.memset(ones[:, :], 1.0).then_inc(ones_set, 1)
            gp.wait_ge(ones_set, 1)

            def squares(norm, src, chunks, at_):
                prev = {"n1": None, "nq": "n1", "nkv": "nq", "nx": "nkv", "nf": "nx", "nz": "nf"}[norm]
                for c in range(chunks):
                    for f in (0, 1):
                        if norm == "n1":
                            gp.wait_ge(val, VAL["x1", c] + 1 if f == 0 else VAL["xs1",] + 1)
                        else:
                            gp.wait_ge(val, VAL[src, c, f] + 1)
                        if c == 0 and prev:
                            full(gp, ("ssq", prev, f))
                        c0, c1 = HALF[f]
                        x = at_(c)[:, c0:c1]
                        if c == 0:
                            step(gp.tensor_tensor(acc[:, c0:c1], x, x, ALU.mult))
                        else:
                            step(gp.tensor_tensor(sq[:, :], x, x, ALU.mult))
                            ins = gp.tensor_tensor(acc[:, c0:c1], acc[:, c0:c1], sq[:, :], ALU.add)
                            if c == chunks - 1:
                                ins.then_inc(sums, 1)
                                done[0] += 1
                                gp.wait_ge(sums, done[0])
                            else:
                                step(ins)

            squares("n1", "x1", KD, lambda c: xT[:, c, :])
            full(gp, ("in", 0, 0))
            gp.memset(up[:, :, 0:NST], 0.0).then_inc(pads_set, 1)
            gp.wait_ge(pads_set, 1)
            squares("nq", "cq", 3, lambda c: cq[:, c, :])
            squares("nkv", "ckv", 2, lambda c: cT[:, c, :])
            gp.wait_ge(ids_in, 16 * NPG)
            gp.wait_ge(rope_in, 16 * 3)
            gp.tensor_scalar(row_ids[:, :], page_ids[:, :], float(PAGE // TPP), row_in_page[:, 0:1],
                             ALU.mult, ALU.add).then_inc(rows_known, 1)
            gp.wait_ge(rows_known, 1)
            full(gp, ("in", 9, 1))
            for i, t in enumerate((qr_hi, qr_lo)):
                for h in range(NH):
                    r0 = RP * (1 - h % 2)
                    gp.memset(t[r0:r0 + RP, h, :].bitcast(F32), 0.0).then_inc(pads_set, 1)
                    gp.wait_ge(pads_set, NH * i + h + 2)
            for g in range(4):
                gp.wait_ge(val, VAL["up", g, 1] + 1)
                if g:
                    gp.wait_ge(val, VAL["pm", g - 1] + 1)
                src = up[:, g, :]
                n = NST + T
                for lvl in range(g + 1):
                    d = 1 << lvl
                    dst = (ws1, ws2)[(g - lvl) % 2]
                    ins = gp.tensor_tensor(dst[:, 2 * d - 1:n], src[:, 2 * d - 1:n], src[:, d - 1:n - d], ALU.add)
                    if lvl == g:
                        ins.then_inc(winsum, 1)
                        gp.wait_ge(winsum, g + 1)
                    else:
                        step(ins)
                    src = dst
            c_rows = a["cache_kv_latent"][0].rearrange("n (p j) r -> (n p) (j r)", j=TPP)
            r_rows = a["cache_k_rope"][0].rearrange("n (p j) r -> (n p) (j r)", j=TPP)
            for b in range(NB):
                if b == 0:
                    gp.wait_ge(lo, SPLIT["pm", 3] + 1)
                    full(gp, ("ut",))
                elif b == 2:
                    gp.wait_ge(own_set, 2)
                    gp.wait_ge(stored, 16 * 7)
                    freed(gp, ("snew",))
                elif b == 3:
                    full(gp, ("ql", NH - 1, 1))
                    gp.memset(q_diag[:, :, :, :, :], 0.0).then_inc(q_zero, 1)
                    full(gp, ("s", NH - 1, 3))
                elif b == 4:
                    full(gp, ("pv", NH - 1, 1))
                elif b == NB - 1:
                    full(gp, ("uv", NH - 1))
                    gp.wait_ge(val, VAL["turned", 0] + 1)
                for dst, src in ((past_c[b], c_rows), (past_r[b], r_rows)):
                    n = src.shape[1]
                    gp.indirect_dma_start(dst.rearrange("p j r -> p (j r)") , None, src[:, :],
                                          bass.IndirectOffsetOnAxis(row_ids[:, :][:, b:b + 1], 0)).then_inc(c_in[b], 16)
            full(gp, ("sc", NB - 1))
            gp.memset(P_pad[:, :], 0.0).then_inc(pad_set, 1)
            squares("nx", "xo1", KD, lambda c: xT[:, c, :])
            squares("nf", "xo2", KD, lambda c: xT[:, c, :])
            squares("nz", "xo3", KD, lambda c: xT[:, c, :])

        @block.scalar
        def _(act):
            splits = [0]

            def split_w(s):
                if s >= NSLOT:
                    return
                act.wait_ge(w_loaded[s % RAW], landed[s])
                if s >= SPL:
                    used(act, s - SPL)
                for c0, c1 in pieces(s):
                    act.activation(whi[:, s % SPL, c0:c1], wraw[:, s % RAW, c0:c1], ACT.Copy).then_inc(w_hi, 1)

            def high(key, dst, src, scale=1.0):
                assert SPLIT[key] == splits[0], key
                splits[0] += 1
                act.activation(dst, src, ACT.Copy, scale=scale).then_inc(hi, 1)

            def after(key):
                act.wait_ge(val, VAL[key] + 1)

            def stage(key, dst, src):
                frees(act.activation(dst, src, ACT.Copy), key)

            def roots(norm, t):
                after(("ms", norm) if norm == "mem" else ("ms", norm, 1))
                act.activation(t, t, ACT.Sqrt).then_inc(root, 1)

            split_w(0)
            after(("gT",))
            for c in range(KD):
                after(("x1", c))
                high(("x1", c), B_hi[:, c, 0:TP], xT[:, c, 0:TP], gain(G_MIX + c))
            after(("xs1",))
            for c in range(KD - 1):
                act.activation(B_hi[:, c, TP:T], xT[:, c, TP:T], ACT.Copy, scale=gain(G_MIX + c))
            high(("xs1",), B_hi[:, KD - 1, TP:T], xT[:, KD - 1, TP:T], gain(G_MIX + KD - 1))
            split_w(1)
            for h in range(NH):
                high(("wuk", h), wuk_hi[:, h, :], full(act, ("wuk", h))[:, 0:KVL])
            for m in range(10):
                split_w(S_IN + m + 2)
                if m == 0:
                    roots("n1", rstd[:, :])
                if m == 7:
                    roots("nq", rstd_q[:, :])
                if m == 8:
                    roots("nkv", rstd_kv[:, :])
                if m < 3:
                    for f, (c0, c1) in enumerate(HALF):
                        after(("cq", m, f))
                        high(("cq", m, f), cqg_hi[:, m, c0:c1], cq[:, m, c0:c1], gain(G_Q + m))
                if m == 6:
                    for f, (c0, c1) in enumerate(PROMPT):
                        after(("kr", f))
                        high(("kr", f), kr_hi[:, c0:c1], kr[:, c0:c1])
                if m == 8:
                    for f, (c0, c1) in enumerate(PROMPT):
                        for r in (0, 1):
                            after(("c", r, f))
                            high(("c", r, f), cT_hi[:, r, c0:c1], cT[:, r, c0:c1])
            for h in range(NH):
                if h % 2 == 0:
                    split_w(S_UQ + h // 2 + 2)
                for f, (c0, c1) in enumerate(HALF):
                    after(("qn", h, f))
                    high(("qn", h, f), A_hi[:, h, c0:c1], tmp[:, 2 * (h % 2) + f, :])
            split_w(S_UQ + 4)
            for g in range(4):
                after(("pm", g))
                high(("pm", g), pm_hi[g][:, :], pm[:, :])
            split_w(S_POOL + 2)
            for g in range(4):
                for f, (c0, c1) in enumerate(HALF):
                    high(("py", g, f), A_hi[:, 4 + g, c0:c1], full(act, ("py", g, f))[:, 0:TH], gain(G_PS + g))
                if g < 2:
                    act.wait_ge(pads_set, 9)
                    for f, (c0, c1) in enumerate(HALF):
                        after(("qr", g, f))
                        act.activation(qr_hi[0:RP, 2 * g, c0:c1], qx[0:RP, g, c0:c1], ACT.Copy)
                        high(("qr", g, f), qr_hi[RP:P, 2 * g + 1, c0:c1], qx[RP:P, g, c0:c1])
            for t in range(4):
                stage(("ct", t), c_nat[:, t, :], full(act, ("ct", t))[:, 0:KVL])
            stage(("kt",), kr_nat[:, :, :], full(act, ("kt",))[:, 0:4 * RP].rearrange("p (t r) -> p t r", t=4))
            stage(("smp",), smp_nat[0:NB, :], full(act, ("smp",))[0:NB, 0:KVL + RP])
            stage(("us",), us_nat[0:NB, :], full(act, ("us",))[0:NB, :])
            stage(("ut",), ut_nat[0:NST, :], full(act, ("ut",))[0:NST, :])
            for t in range(4):
                freed(act, ("ct", t))
                high(("cn", t), cn_hi[:, t, :], c_nat[:, t, :])
            act.dma_start(o_kvp[0, 0].rearrange("(t p) r -> p t r", p=P), c_nat[:, :, :]).then_inc(stored, 16)
            freed(act, ("kt",))
            act.dma_start(o_krp[0, 0].rearrange("(t p) r -> p t r", p=P), kr_nat[:, :, :]).then_inc(stored, 16)
            freed(act, ("smp",))
            act.dma_start(o_kvs[0].rearrange("b t r -> (b t) r"), smp_nat[0:NB, 0:KVL]).then_inc(stored, 16)
            act.dma_start(o_krs[0].rearrange("b t r -> (b t) r"), smp_nat[0:NB, KVL:KVL + RP]).then_inc(stored, 16)
            freed(act, ("us",))
            act.dma_start(o_pools[0, :, NST - 1, :], us_nat[0:NB, :]).then_inc(stored, 16)
            freed(act, ("ut",))
            act.dma_start(o_poolp[0, 0], ut_nat[0:NST, :]).then_inc(stored, 16)
            for r in (0, 1):
                high(("ql", 0, r), ql_hi[:, r, :], full(act, ("ql", 0, r)))

            split_w(S_UV + 2)
            us = units()

            def exps(n):
                h, i = us[n]
                b = full(act, ("s", h, i))
                after(("negm", h, i))
                frees(act.activation(prob[i][:, :], b[:, 0:(i + 1) * P], ACT.Exp, bias=stat[:, 1, i:i + 1],
                                     scale=MLA_SCALE, accum_out=stat[:, 2, i:i + 1]), ("s", h, i))

            exps(0)
            exps(1)
            for n, (h, i) in enumerate(us):
                b = full(act, ("pt", h, i))
                high(("pt", h, i), PT_hi[:, 0:i + 1, i * P:(i + 1) * P],
                     b[:, 0:(i + 1) * P].rearrange("p (j q) -> p j q", j=i + 1))
                if n + 2 < len(us):
                    exps(n + 2)
                if i == 0 and h + 1 < NH:
                    for r in (0, 1):
                        high(("ql", h + 1, r), ql_hi[:, r, :], full(act, ("ql", h + 1, r)))
                if i == 0 and h:
                    high(("uv", h - 1), A_hi[:, h - 1, 0:TP], full(act, ("uv", h - 1)))
                if i == 3:
                    for r in (0, 1):
                        high(("pv", h, r), ol_hi[:, r, :], full(act, ("pv", h, r)))
            high(("uv", NH - 1), A_hi[:, NH - 1, 0:TP], full(act, ("uv", NH - 1)))

            stage(("own",), own_nat[0:SQ, :], full(act, ("own",))[0:SQ, 0:KVL])
            after(("bias",))
            act.activation(S[:, :, :], S[:, :, :], ACT.Exp, bias=srow[:, 5:6], scale=MLA_SCALE,
                           accum_out=srow[:, 6:7]).then_inc(s_exp, 1)
            act.activation(srow[0:SQ, 8:9], srow[0:SQ, 7:8], ACT.Exp, bias=srow[0:SQ, 5:6], scale=MLA_SCALE).then_inc(s_exp, 1)
            high(("ot",), ols_hi[:, :, :, :], full(act, ("ot",))[:, 0:2 * SQ].rearrange("p (r b h) -> p r h b", r=2, b=NB))
            high(("uvs",), A_hi[:, 0:NH, TP:T], full(act, ("uvs",))[:, 0:NH * NB].rearrange("p (h b) -> p h b", h=NH))

            for m in range(KD):
                split_w(S_OUT + m + 2)
                if m == 1:
                    act.wait_ge(mem_in, 32)
                    for t in (0, 1):
                        act.activation(m_sq[:, t, :], m_nat[:, t, :], ACT.Square, accum_out=mem_ss[:, t:t + 1]).then_inc(mem_sq, 1)
                for f, (c0, c1) in enumerate(HALF):
                    after(("xo1", m, f))
                    high(("xo1", m, f), B_hi[:, m, c0:c1], xT[:, m, c0:c1], gain(G_X + m))
                if m == 1:
                    roots("mem", mem_ss[:, 2:4])
                    for k in range(4):
                        b = full(act, ("mt", k))
                        act.activation(mT_hi[:, 2 * k, :], b[:, 0:NMEM], ACT.Copy, scale=gain(G_MEM + 2 * k))
                        high(("mt", k), mT_hi[:, 2 * k + 1, :], b[:, NMEM:2 * NMEM], gain(G_MEM + 2 * k + 1))

            def rows(n):
                b = full(act, ("mn", n)).rearrange("p (t c) -> p t c", t=2)
                if n == 4:
                    act.wait_ge(kv_st, 16)
                j = n % 4
                stage(("mn", n), kv_nat[:, :, j * 2 * P:(j + 1) * 2 * P], b)
                if n >= 4:
                    freed(act, ("mn", n))
                    high(("mn", n), mvn_hi[:, :, j * 2 * P:(j + 1) * 2 * P], kv_nat[:, :, j * 2 * P:(j + 1) * 2 * P])
                if j == 3:
                    freed(act, ("mn", n))
                    dst = (o_mk, o_mv)[n // 4][0, 0].rearrange("(t p) h d -> p t (h d)", p=P)
                    act.dma_start(dst, kv_nat[:, :, :]).then_inc(kv_st, 16)

            for j in range(16):
                split_w(S_MK + j + 2)
                if 4 <= j < 12:
                    act.wait_ge(lo, SPLIT["mm", j - 4] + 1)
                stage(("mm", j), kv_T[:, j % 4, :], full(act, ("mm", j))[:, 0:NMEM])
                if j < 8:
                    freed(act, ("mm", j))
                    high(("mm", j), mkT_hi[:, j, :], kv_T[:, j % 4, :])
                if j >= 2 and j % 2 == 0:
                    rows(j // 2 - 1)
            rows(7)

            for m in range(KD):
                split_w(S_XQ + m + 2)
                if m == 0:
                    roots("nx", rstd[:, :])
                for f, (c0, c1) in enumerate(PROMPT):
                    after(("xq", m, f))
                    high(("xq", m, f), q_hi[:, m, c0:c1], tmp[:, 2 * (m % 2) + f, 0:c1 - c0])

            def cexps(h):
                after(("cnegm", h))
                for ip in (0, 1):
                    b = full(act, ("cs", h, ip))
                    for i in (0, 1):
                        c = 2 * ip + i
                        ins = act.activation(Pc[:, h % 2, ip, i, :], b[:, i * NMEM:(i + 1) * NMEM], ACT.Exp,
                                             bias=cstat[:, 1, h % 2, c:c + 1], scale=MEM_SCALE,
                                             accum_out=cstat[:, 2, h % 2, c:c + 1])
                    frees(ins, ("cs", h, ip))

            act.wait_ge(kv_st, 32)
            cexps(0)
            for h in range(NH):
                if h + 1 < NH:
                    cexps(h + 1)
                for mb in (0, 1):
                    high(("cpt", h, mb), PTc_hi[:, mb, :], full(act, ("cpt", h, mb)))
                for dc in (0, 1):
                    high(("cpv", h, dc), A_hi[:, 2 * h + dc, 0:TP], full(act, ("cpv", h, dc)))
            after(("cdif",))
            act.activation(Pcs[:, :, :, :], Dc[:, :, :, :], ACT.Exp, scale=MEM_SCALE).then_inc(c_exp, 1)
            act.wait_ge(v_used, NB)
            high(("co",), A_hi[:, :, TP:T], accO[:, 0:KD * NB].rearrange("p (j b) -> p j b", j=KD))

            for m in range(KD):
                split_w(S_XO + m + 2)
                for f, (c0, c1) in enumerate(HALF):
                    after(("xo2", m, f))
                    high(("xo2", m, f), B_hi[:, m, c0:c1], xT[:, m, c0:c1], gain(G_FFN + m))

            for j in range(NF):
                split_w(S_FFN + 2 * j + 2)
                split_w(S_FFN + 2 * j + 3)
                if j == 0:
                    roots("nf", rstd[:, :])
                for f, (c0, c1) in enumerate(HALF):
                    after(("gv", j, f))
                    act.activation(sig[:, f, :], gate[:, f, :], ACT.Sigmoid).then_inc(sig_set, 1)
                for f, (c0, c1) in enumerate(HALF):
                    after(("h", j, f))
                    high(("h", j, f), h_hi[:, j, c0:c1], hv[:, f, :])
            for s in range(S_DOWN + 2, NSLOT):
                split_w(s)
            roots("nz", rstd[:, :])

            for t in range(5):
                n = P if t < 4 else NB
                if t >= 2:
                    act.wait_ge(y_st[t % 2], 16 * (t // 2))
                for k in (0, 1):
                    stage(("y", t, k), y_nat[0:n, t % 2, k * 512:(k + 1) * 512], full(act, ("y", t, k))[0:n, :])
                for k in (0, 1):
                    freed(act, ("y", t, k))
                dst = y_p[0, t * P:(t + 1) * P, :] if t < 4 else y_s.rearrange("b t d -> (b t) d")
                act.dma_start(dst, y_nat[0:n, t % 2, :]).then_inc(y_st[t % 2], 16)
            assert splits[0] == len(SPLIT.at)

        @block.vector
        def _(dve):
            steps, splits, vals = [0], [0], [0]

            def step(ins):
                steps[0] += 1
                ins.then_inc(dve_step, 1)
                dve.wait_ge(dve_step, steps[0])

            def value(key, ins):
                assert VAL[key] == vals[0], key
                vals[0] += 1
                ins.then_inc(val, 1)

            def own(key):
                dve.wait_ge(val, VAL[key] + 1)

            def settle():
                dve.wait_ge(val, vals[0])
                if splits[0]:
                    dve.wait_ge(lo, splits[0])

            def rest(dst, src, high, g=None):
                if g is None:
                    return dve.tensor_tensor(dst, src, high.bitcast(F32), ALU.subtract)
                return dve.scalar_tensor_tensor(dst, src, g, high.bitcast(F32), ALU.mult, ALU.subtract)

            def low(key, dst, src, high, g=None):
                assert SPLIT[key] == splits[0], key
                splits[0] += 1
                dve.wait_ge(hi, SPLIT[key] + 1)
                rest(dst, src, high, g).then_inc(lo, 1)

            def split_w(s):
                if s >= NSLOT:
                    return
                for i, (c0, c1) in enumerate(pieces(s)):
                    dve.wait_ge(w_hi, 2 * s + i + 1)
                    rest(wlo[:, s % SPL, c0:c1], wraw[:, s % RAW, c0:c1], whi[:, s % SPL, c0:c1]).then_inc(w_lo, 1)

            def inverse_rms(norm, width, dst):
                for f, (c0, c1) in enumerate(HALF):
                    b = full(dve, ("ssq", norm, f))
                    value(("ms", norm, f), dve.tensor_scalar(dst[:, c0:c1], b[:, 0:TH], 1.0 / width, EPS, ALU.mult, ALU.add))
                dve.wait_ge(root, ROOTS.index(norm) + 1)
                step(dve.reciprocal(dst[:, :], dst[:, :]))

            def add_residual(key, out_key, m, f):
                c0, c1 = HALF[f]
                b = full(dve, key)
                settle()
                ins = dve.tensor_tensor(xT[:, m, c0:c1], b[:, 0:TH], xT[:, m, c0:c1], ALU.add)
                value(out_key, ins)

            def scaled(key, dst, r, f, out_key):
                c0, c1 = HALF[f]
                b = full(dve, key)
                settle()
                ins = dve.tensor_tensor(dst, b[:, 0:TH], r[:, c0:c1], ALU.mult)
                value(out_key, ins)

            step(dve.memset(qrs[:, :, :], 0.0))
            ins = dve.tensor_copy(gT[:, 0:NG], full(dve, ("gain",))[:, 0:NG])
            value(("gT",), ins)
            own(("gT",))
            b = full(dve, ("xs",))
            ins = dve.tensor_copy(xT[:, :, TP:T], b[:, 0:KD * NB].rearrange("p (c n) -> p c n", c=KD))
            value(("xs1",), ins)
            for c in range(KD):
                ins = dve.tensor_copy(xT[:, c, 0:TP], full(dve, ("xt", c)))
                value(("x1", c), ins)
                if c:
                    low(("x1", c - 1), B_lo[:, c - 1, 0:TP], xT[:, c - 1, 0:TP], B_hi[:, c - 1, 0:TP], gain(G_MIX + c - 1))
            low(("x1", KD - 1), B_lo[:, KD - 1, 0:TP], xT[:, KD - 1, 0:TP], B_hi[:, KD - 1, 0:TP], gain(G_MIX + KD - 1))
            dve.wait_ge(hi, SPLIT["xs1",] + 1)
            for c in range(KD - 1):
                rest(B_lo[:, c, TP:T], xT[:, c, TP:T], B_hi[:, c, TP:T], gain(G_MIX + c))
            low(("xs1",), B_lo[:, KD - 1, TP:T], xT[:, KD - 1, TP:T], B_hi[:, KD - 1, TP:T], gain(G_MIX + KD - 1))
            split_w(0)
            split_w(1)
            ins = dve.tensor_copy(cp_T[:, :, :], full(dve, ("cp",))[:, 0:4 * NB * NST].rearrange("p (g n) -> p g n", g=4))
            value(("cpT",), ins)
            for h in range(NH):
                low(("wuk", h), wuk_lo[:, h, :], full(dve, ("wuk", h))[:, 0:KVL], wuk_hi[:, h, :])

            def rope(x, dst, rot_key, f, out_key):
                c0, c1 = HALF[f]
                b = full(dve, rot_key)
                settle()
                dve.tensor_tensor(tmp[:, 0, :], x[:, c0:c1], rope_c[:, c0:c1], ALU.mult)
                frees(dve.tensor_tensor(tmp[:, 1, :], b[:, 0:TH], rope_s[:, c0:c1], ALU.mult), rot_key)
                freed(dve, rot_key)
                value(out_key, dve.tensor_tensor(dst[:, c0:c1], tmp[:, 0, :], tmp[:, 1, :], ALU.add))

            for m in range(10):
                split_w(S_IN + m + 2)
                if m == 0:
                    inverse_rms("n1", D, rstd)
                for f, (c0, c1) in enumerate(HALF):
                    if m < 3:
                        dst, key = cq[:, m, c0:c1], ("cq", m, f)
                    elif m < 5:
                        dst, key = cT[:, m - 3, c0:c1], ("ckv", m - 3, f)
                    elif m == 5:
                        dst, key = krx[:, c0:c1], ("krx", f)
                    else:
                        dst, key = up[:, m - 6, NST + c0:NST + c1], ("up", m - 6, f)
                    scaled(("in", m, f), dst, rstd, f, key)
                if m < 3:
                    for f, (c0, c1) in enumerate(HALF):
                        low(("cq", m, f), cqg_lo[:, m, c0:c1], cq[:, m, c0:c1], cqg_hi[:, m, c0:c1], gain(G_Q + m))
                if m == 6:
                    dve.wait_ge(rope_in, 48)
                    for f, (c0, c1) in enumerate(PROMPT):
                        rope(krx, kr, ("rotk", f), f, ("kr", f))
                    for f, (c0, c1) in enumerate(PROMPT):
                        low(("kr", f), kr_lo[:, c0:c1], kr[:, c0:c1], kr_hi[:, c0:c1])
                if m == 7:
                    inverse_rms("nq", QL, rstd_q)
                if m == 8:
                    inverse_rms("nkv", KVL, rstd_kv)
                    settle()
                    for f, (c0, c1) in enumerate(HALF):
                        for r in (0, 1):
                            value(("c", r, f), dve.scalar_tensor_tensor(cT[:, r, c0:c1], cT[:, r, c0:c1], gain(G_KV + r),
                                                                        rstd_kv[:, c0:c1], ALU.mult, ALU.mult))
                    for f, (c0, c1) in enumerate(PROMPT):
                        for r in (0, 1):
                            low(("c", r, f), cT_lo[:, r, c0:c1], cT[:, r, c0:c1], cT_hi[:, r, c0:c1])
            for h in range(NH):
                if h % 2 == 0:
                    split_w(S_UQ + h // 2 + 2)
                for f in (0, 1):
                    scaled(("un", h, f), tmp[:, 2 * (h % 2) + f, :], rstd_q, f, ("qn", h, f))
                for f, (c0, c1) in enumerate(HALF):
                    low(("qn", h, f), A_lo[:, h, c0:c1], tmp[:, 2 * (h % 2) + f, :], A_hi[:, h, c0:c1])
            split_w(S_UQ + 4)
            for p in (0, 1):
                for f, (c0, c1) in enumerate(HALF):
                    scaled(("ur", p, f), qx[:, p, c0:c1], rstd_q, f, ("qx", p, f))
            for g, win in enumerate(WINDOWS):
                x, ws = up[:, g, NST:NST + T], ws1[:, NST:NST + T]
                dve.wait_ge(winsum, g + 1)
                settle()
                own(("up", g, 1))
                step(dve.scalar_tensor_tensor(pm[:, 0:TP], ws[:, 0:TP], 1.0 / win, x[:, 0:TP], ALU.mult, ALU.subtract))
                c = slice(0, win - 1)
                step(dve.tensor_tensor(ps_[:, 1:3, :].rearrange("p a b -> p (a b)")[:, c], ws[:, c], rcnt[:, g, c], ALU.mult))
                dve.tensor_tensor(pm[:, c], ps_[:, 1:3, :].rearrange("p a b -> p (a b)")[:, c], x[:, c], ALU.subtract)
                old = cp_T[:, g, :].rearrange("p (b t) -> p b t", b=NB)[:, :, NST - win + 1:NST]
                step(dve.tensor_reduce(ps_[:, 0, :], old, AX, ALU.add))
                step(dve.tensor_tensor(ps_[:, 0, :], ps_[:, 0, :], x[:, TP:T], ALU.add))
                value(("pm", g), dve.scalar_tensor_tensor(pm[:, TP:T], ps_[:, 0, :], 1.0 / win, x[:, TP:T], ALU.mult, ALU.subtract))
                low(("pm", g), pm_lo[g][:, :], pm[:, :], pm_hi[g][:, :])
            split_w(S_POOL + 2)
            for g in range(4):
                for f, (c0, c1) in enumerate(HALF):
                    low(("py", g, f), A_lo[:, 4 + g, c0:c1], full(dve, ("py", g, f))[:, 0:TH], A_hi[:, 4 + g, c0:c1],
                        gain(G_PS + g))
                if g < 2:
                    for f in (0, 1):
                        rope(qx[:, g, :], qx[:, g, :], ("rotq", g, f), f, ("qr", g, f))
                    own(("qr", g, 1))
                    for h in (0, 1):
                        dve.tensor_copy(qrs[0:RP, :, 2 * g + h], qx[RP * h:RP * h + RP, g, TP:T])
                    for f, (c0, c1) in enumerate(HALF):
                        dve.wait_ge(hi, SPLIT["qr", g, f] + 1)
                        rest(qr_lo[0:RP, 2 * g, c0:c1], qx[0:RP, g, c0:c1], qr_hi[0:RP, 2 * g, c0:c1])
                        low(("qr", g, f), qr_lo[RP:P, 2 * g + 1, c0:c1], qx[RP:P, g, c0:c1], qr_hi[RP:P, 2 * g + 1, c0:c1])
            for t in range(4):
                low(("cn", t), cn_lo[:, t, :], c_nat[:, t, :], cn_hi[:, t, :])
            ins = dve.tensor_copy(qls[:, :, :, :], full(dve, ("qls",))[:, 0:2 * NH * NB].rearrange("p (r h b) -> p r h b", r=2, h=NH))
            value(("qls",), ins)
            own(("qls",))
            def over_heads(x):
                return x.unsqueeze(2).to_broadcast([P, NB, NH])
            dve.tensor_tensor(cols[:, 0], qls[:, 0].rearrange("p h b -> p b h"), over_heads(cT[:, 0, TP:T]), ALU.mult)
            dve.tensor_tensor(cols[:, 1], qls[:, 1].rearrange("p h b -> p b h"), over_heads(cT[:, 1, TP:T]), ALU.mult)
            step(dve.tensor_tensor(cols[:, 2], qrs[:, :, :], over_heads(kr[:, TP:T]), ALU.mult))
            step(dve.tensor_tensor(cols[:, 0], cols[:, 0], cols[:, 1], ALU.add))
            value(("sprod",), dve.tensor_tensor(cols[:, 0], cols[:, 0], cols[:, 2], ALU.add))
            for r in (0, 1):
                dve.tensor_copy(own_c[:, r], over_heads(cT[:, r, TP:T])).then_inc(own_set, 1)
            for r in (0, 1):
                low(("ql", 0, r), ql_lo[:, r, :], full(dve, ("ql", 0, r)), ql_hi[:, r, :])

            split_w(S_UV + 2)
            us = units()

            def maxes(n):
                h, i = us[n]
                b = full(dve, ("s", h, i))
                settle()
                step(dve.tensor_tensor(b[:, i * P:(i + 1) * P], b[:, i * P:(i + 1) * P], mask[:, :], ALU.add))
                step(dve.reduce_max(stat[:, 0, i:i + 1], b[:, 0:(i + 1) * P], AX))
                value(("negm", h, i), dve.tensor_scalar(stat[:, 1, i:i + 1], stat[:, 0, i:i + 1], -MLA_SCALE, None, ALU.mult))

            def normalise(n):
                h, i = us[n]
                freed(dve, ("s", h, i))
                step(dve.reciprocal(stat[:, 3, i:i + 1], stat[:, 2, i:i + 1]))
                value(("pn", h, i), dve.tensor_scalar(prob[i][:, :], prob[i][:, :], stat[:, 3, i:i + 1], None, ALU.mult))

            def spread_queries(i):
                if i == 0:
                    dve.wait_ge(q_zero, 1)
                for k in range(P // SQ):
                    src = qls[SQ * k:SQ * (k + 1)].rearrange("p r h b -> p r b h")
                    dve.tensor_copy(q_diag[SQ * i:SQ * (i + 1), k:KVL // SQ:P // SQ, i, :, :], src).then_inc(q_built, 1)
                for k in range(RP // SQ):
                    dve.tensor_copy(q_diag[SQ * i:SQ * (i + 1), KVL // SQ + k, i, :, :],
                                    qrs[SQ * k:SQ * (k + 1)]).then_inc(q_built, 1)

            maxes(0)
            maxes(1)
            normalise(0)
            dve.wait_ge(stored, 16 * 7)
            for n, (h, i) in enumerate(us):
                if n + 1 < len(us):
                    normalise(n + 1)
                if n + 2 < len(us):
                    maxes(n + 2)
                b = full(dve, ("pt", h, i))
                low(("pt", h, i), PT_lo[:, 0:i + 1, i * P:(i + 1) * P],
                    b[:, 0:(i + 1) * P].rearrange("p (j q) -> p j q", j=i + 1),
                    PT_hi[:, 0:i + 1, i * P:(i + 1) * P])
                if i == 0 and h + 1 < NH:
                    for r in (0, 1):
                        low(("ql", h + 1, r), ql_lo[:, r, :], full(dve, ("ql", h + 1, r)), ql_hi[:, r, :])
                if i == 0 and h:
                    low(("uv", h - 1), A_lo[:, h - 1, 0:TP], full(dve, ("uv", h - 1)), A_hi[:, h - 1, 0:TP])
                if i == 3:
                    for r in (0, 1):
                        low(("pv", h, r), ol_lo[:, r, :], full(dve, ("pv", h, r)), ol_hi[:, r, :])
                if len(us) - 6 <= n < len(us) - 2:
                    spread_queries(n - len(us) + 6)
                if n == 0:
                    frees(dve.tensor_copy(srow[0:SQ, 7:8], full(dve, ("snew",))[0:SQ, 0:1]), ("snew",))
            low(("uv", NH - 1), A_lo[:, NH - 1, 0:TP], full(dve, ("uv", NH - 1)), A_hi[:, NH - 1, 0:TP])

            groups = [slice(SQ * i, SQ * (i + 1)) for i in range(P // SQ)]

            def gather_rows(column):
                for i, g in enumerate(groups):
                    ins = dve.tensor_copy(srow[0:SQ, i:i + 1], srow[g, column:column + 1])
                step(ins)

            def turn(b):
                dve.wait_ge(c_in[b], 32)
                if b >= 2:
                    full(dve, ("sc", b - 2))
                else:
                    full(dve, ("s", NH - 1, 3))
                dve.transpose(turned_c[:, b % 2].rearrange("p j k t -> p (j k t)"), past_c[b].rearrange("p j r -> p (j r)"))
                value(("turned", b), dve.transpose(turned_r[:, b % 2].rearrange("p j k t -> p (j k t)"),
                                                   past_r[b].rearrange("p j r -> p (j r)")))

            def own_scores(b):
                x = full(dve, ("sc", b))[:, 0:TPP * SQ].rearrange("p (j t) -> p j t", j=TPP)
                m = is_sample[:, b:b + 1]
                if b == 0:
                    ins = dve.tensor_scalar(S[:, :, :], x, m, None, ALU.mult)
                else:
                    ins = dve.scalar_tensor_tensor(S[:, :, :], x, m, S[:, :, :], ALU.mult, ALU.add)
                frees(ins, ("sc", b))
                freed(dve, ("sc", b))

            turn(0)
            turn(1)
            for b in range(NB):
                own_scores(b)
                if b + 2 < NB:
                    turn(b + 2)
            freed(dve, ("snew",))
            step(dve.tensor_reduce(srow[:, 4:5], S[:, :, :].rearrange("p j t -> p (j t)"), AX, ALU.max))
            gather_rows(4)
            step(dve.reduce_max(srow[0:SQ, 9:10], srow[0:SQ, 0:4], AX))
            step(dve.tensor_tensor(srow[0:SQ, 9:10], srow[0:SQ, 9:10], srow[0:SQ, 7:8], ALU.max))
            step(dve.tensor_scalar(srow[0:SQ, 10:11], srow[0:SQ, 9:10], -MLA_SCALE, None, ALU.mult))
            for g in groups:
                ins = dve.tensor_copy(srow[g, 5:6], srow[0:SQ, 10:11])
            value(("bias",), ins)
            dve.wait_ge(s_exp, 2)
            value(("own_p",), dve.tensor_scalar(diag[0:SQ, :], ident[0:SQ, 0:SQ], srow[0:SQ, 8:9], None, ALU.mult))
            step(dve.transpose(PT[:, :, :, :].rearrange("p j b h -> p (j b h)"), S[:, :, :].rearrange("p j t -> p (j t)")))
            dve.wait_ge(pad_set, 1)
            pad = P_pad[:, :].rearrange("p (b x) -> p b x", x=PS)[:, :, 0:TPP * SQ].rearrange("p b (j c) -> p b j c", c=SQ)
            value(("spread_p",), dve.tensor_copy(pad[:, :, :, 0:NH], PT[:, :, :, :].rearrange("p j b h -> p b j h")))
            gather_rows(6)
            step(dve.tensor_reduce(srow[0:SQ, 9:10], srow[0:SQ, 0:4], AX, ALU.add))
            step(dve.tensor_tensor(srow[0:SQ, 9:10], srow[0:SQ, 9:10], srow[0:SQ, 8:9], ALU.add))
            step(dve.reciprocal(srow[0:SQ, 10:11], srow[0:SQ, 9:10]))
            dve.wait_ge(past_mixed, 1)
            value(("rows",), dve.tensor_scalar(o_rows[0:SQ, :], accO[0:SQ, 0:KVL], srow[0:SQ, 10:11], None, ALU.mult))
            low(("ot",), ols_lo[:, :, :, :], full(dve, ("ot",))[:, 0:2 * SQ].rearrange("p (r b h) -> p r h b", r=2, b=NB),
                ols_hi[:, :, :, :])
            low(("uvs",), A_lo[:, 0:NH, TP:T], full(dve, ("uvs",))[:, 0:NH * NB].rearrange("p (h b) -> p h b", h=NH),
                A_hi[:, 0:NH, TP:T])

            def column_max(S, n, mxt, mxb, mx_key, diag_key):
                value(mx_key, dve.tensor_reduce(cols[:, 3], S.rearrange("p b j h -> p b h j"), AX, ALU.max))
                b = full(dve, mxt)
                ins = dve.reduce_max(cols[0:NB * NH, 2].rearrange("p b h -> p (b h)")[:, 0:1], b[0:NB * NH, 0:P], AX)
                frees(ins, mxt)
                freed(dve, mxt)
                value(diag_key, dve.tensor_scalar(diag[0:NB * NH, :], ident[0:NB * NH, 0:NB * NH],
                                                  cols[0:NB * NH, 2].rearrange("p b h -> p (b h)")[:, 0:1], None, ALU.mult))
                b = full(dve, mxb)
                frees(dve.tensor_copy(cols[:, 3].rearrange("p b h -> p (b h)"), b[:, 0:NB * NH]), mxb)
                freed(dve, mxb)

            def inner(x, n):
                return x.unsqueeze(2).to_broadcast([P, NB, n, NH])

            for m in range(KD):
                split_w(S_OUT + m + 2)
                for f in (0, 1):
                    add_residual(("o", m, f), ("xo1", m, f), m, f)
                for f, (c0, c1) in enumerate(HALF):
                    low(("xo1", m, f), B_lo[:, m, c0:c1], xT[:, m, c0:c1], B_hi[:, m, c0:c1], gain(G_X + m))
                if m == 1:
                    dve.wait_ge(mem_sq, 2)
                    value(("ms", "mem"), dve.tensor_scalar(mem_ss[:, 2:4], mem_ss[:, 0:2], 1.0 / D, EPS, ALU.mult, ALU.add))
                    dve.wait_ge(root, ROOTS.index("mem") + 1)
                    step(dve.reciprocal(mem_ss[:, 2:4], mem_ss[:, 2:4]))
                    dve.tensor_scalar(m_nat[:, 0, :], m_nat[:, 0, :], mem_ss[:, 2:3], None, ALU.mult)
                    value(("memn",), dve.tensor_scalar(m_nat[:, 1, :], m_nat[:, 1, :], mem_ss[:, 3:4], None, ALU.mult))
                    for k in range(4):
                        b = full(dve, ("mt", k))
                        dve.wait_ge(hi, SPLIT["mt", k] + 1)
                        rest(mT_lo[:, 2 * k, :], b[:, 0:NMEM], mT_hi[:, 2 * k, :], gain(G_MEM + 2 * k))
                        low(("mt", k), mT_lo[:, 2 * k + 1, :], b[:, NMEM:2 * NMEM], mT_hi[:, 2 * k + 1, :],
                            gain(G_MEM + 2 * k + 1))

            def rows(n):
                if n >= 4:
                    c = slice((n % 4) * 2 * P, (n % 4 + 1) * 2 * P)
                    low(("mn", n), mvn_lo[:, :, c], kv_nat[:, :, c], mvn_hi[:, :, c])

            for j in range(16):
                split_w(S_MK + j + 2)
                if j < 8:
                    low(("mm", j), mkT_lo[:, j, :], kv_T[:, j % 4, :], mkT_hi[:, j, :])
                if j >= 2 and j % 2 == 0:
                    rows(j // 2 - 1)
            rows(7)

            for m in range(KD):
                split_w(S_XQ + m + 2)
                if m == 0:
                    inverse_rms("nx", D, rstd)
                for f in (0, 1):
                    scaled(("xq", m, f), tmp[:, 2 * (m % 2) + f, :], rstd, f, ("xq", m, f))
                own(("xq", m, 1))
                dve.tensor_copy(qcs[:, m, :], tmp[:, 2 * (m % 2) + 1, TH - NB:TH]).then_inc(qcs_set, 1)
                for f, (c0, c1) in enumerate(PROMPT):
                    low(("xq", m, f), q_lo[:, m, c0:c1], tmp[:, 2 * (m % 2) + f, 0:c1 - c0], q_hi[:, m, c0:c1])
            for k in (0, 1):
                frees(dve.tensor_copy(q_nat[0:NB, k * 512:(k + 1) * 512], full(dve, ("qt", k))[0:NB, :]), ("qt", k))

            def cmaxes(h):
                for ip in (0, 1):
                    b = full(dve, ("cs", h, ip)).rearrange("p (i m) -> p i m", i=2)
                    step(dve.reduce_max(cstat[:, 0, h % 2, 2 * ip:2 * ip + 2], b, AX))
                value(("cnegm", h), dve.tensor_scalar(cstat[:, 1, h % 2, :], cstat[:, 0, h % 2, :], -MEM_SCALE, None, ALU.mult))

            def sample_scores(b):
                dve.wait_ge(kv_in[b % K3], 16 * (b // K3 + 1))
                for k in (0, 1):
                    q = full(dve, ("qb", b, k))
                    for h in (2 * k, 2 * k + 1):
                        for m2 in (0, 1):
                            ins = dve.tensor_tensor_reduce(
                                prod[:, :], kv_ring[:, b % K3, m2, h * MD:(h + 1) * MD], q[:, (h % 2) * MD:(h % 2 + 1) * MD],
                                1.0, 0.0, ALU.mult, ALU.add, Sc[:, b, m2, h:h + 1])
                            if (h % 2, m2) != (1, 1):
                                step(ins)
                    frees(ins, ("qb", b, k))
                    freed(dve, ("qb", b, k))

            cmaxes(0)
            for h in range(NH):
                if h + 1 < NH:
                    cmaxes(h + 1)
                for ip in (0, 1):
                    freed(dve, ("cs", h, ip))
                step(dve.reciprocal(cstat[:, 3, h % 2, :], cstat[:, 2, h % 2, :]))
                p4 = Pc[:, h % 2].rearrange("p a b m -> p (a b) m")
                value(("cpn", h), dve.tensor_tensor(p4, p4, cstat[:, 3, h % 2, :].unsqueeze(2).to_broadcast([P, 4, NMEM]), ALU.mult))
                for mb in (0, 1):
                    low(("cpt", h, mb), PTc_lo[:, mb, :], full(dve, ("cpt", h, mb)), PTc_hi[:, mb, :])
                sample_scores(2 * h)
                for dc in (0, 1):
                    low(("cpv", h, dc), A_lo[:, 2 * h + dc, 0:TP], full(dve, ("cpv", h, dc)), A_hi[:, 2 * h + dc, 0:TP])
                sample_scores(2 * h + 1)
            column_max(Sc[:, :, :, :], 2, ("cmxt",), ("cmxb",), ("cmx",), ("cdiag",))
            value(("cdif",), dve.tensor_tensor(Dc[:, :, :, :], Sc[:, :, :, :], inner(cols[:, 3], 2), ALU.subtract))
            dve.wait_ge(c_exp, 1)
            value(("csum",), dve.tensor_reduce(cols[:, 6], Pcs[:, :, :, :].rearrange("p b j h -> p b h j"), AX, ALU.add))
            ins = dve.reciprocal(cols[:, 7].rearrange("p b h -> p (b h)"), full(dve, ("ctot",))[:, 0:NB * NH])
            frees(ins, ("ctot",))
            freed(dve, ("ctot",))
            value(("cpnorm",), dve.tensor_tensor(Pcs[:, :, :, :], Pcs[:, :, :, :], inner(cols[:, 7], 2), ALU.mult))
            low(("co",), A_lo[:, :, TP:T], accO[:, 0:KD * NB].rearrange("p (j b) -> p j b", j=KD), A_hi[:, :, TP:T])

            for m in range(KD):
                split_w(S_XO + m + 2)
                for f in (0, 1):
                    add_residual(("xo", m, f), ("xo2", m, f), m, f)
                for f, (c0, c1) in enumerate(HALF):
                    low(("xo2", m, f), B_lo[:, m, c0:c1], xT[:, m, c0:c1], B_hi[:, m, c0:c1], gain(G_FFN + m))

            for j in range(NF):
                split_w(S_FFN + 2 * j + 2)
                split_w(S_FFN + 2 * j + 3)
                if j == 0:
                    inverse_rms("nf", D, rstd)
                for f in (0, 1):
                    scaled(("g", j, f), gate[:, f, :], rstd, f, ("gv", j, f))
                for f, (c0, c1) in enumerate(HALF):
                    b = full(dve, ("u", j, f))
                    settle()
                    ins = dve.tensor_tensor(upv[:, f, :], b[:, 0:TH], rstd[:, c0:c1], ALU.mult)
                    frees(ins, ("u", j, f))
                    freed(dve, ("u", j, f))
                    step(dve.tensor_tensor(upv[:, f, :], upv[:, f, :], gate[:, f, :], ALU.mult))
                    dve.wait_ge(sig_set, 2 * j + f + 1)
                    value(("h", j, f), dve.tensor_tensor(hv[:, f, :], upv[:, f, :], sig[:, f, :], ALU.mult))
                for f, (c0, c1) in enumerate(HALF):
                    low(("h", j, f), h_lo[:, j, c0:c1], hv[:, f, :], h_hi[:, j, c0:c1])
            for m in range(KD):
                for part in range(3):
                    split_w(S_DOWN + 3 * m + part + 2)
                for f in (0, 1):
                    add_residual(("d", m, f), ("xo3", m, f), m, f)

            inverse_rms("nz", D, rstd)
            for f, (c0, c1) in enumerate(HALF):
                for m in range(KD):
                    value(("yT", m, f), dve.scalar_tensor_tensor(yT[:, m, c0:c1], xT[:, m, c0:c1], gain(G_FIN + m),
                                                                 rstd[:, c0:c1], ALU.mult, ALU.mult))
            assert splits[0] == len(SPLIT.at) and vals[0] == len(VAL.at)

        @block.tensor
        def _(pe):
            uses, order = [0], bank_order()

            def out(key):
                n = BANK[key]
                assert n == uses[0], key
                uses[0] += 1
                if n >= RING:
                    freed(pe, order[n - RING])
                return ps[:, n % RING]

            def filled(ins, key):
                ins.then_inc(bank_full[BANK[key] % RING], 1)

            def after(key):
                pe.wait_ge(val, VAL[key] + 1)

            def split(key):
                pe.wait_ge(lo, SPLIT[key] + 1)

            def weights(s):
                pe.wait_ge(w_lo, 2 * (s + 1))

            def mm3(dst, left, right, first, last):
                pe.matmul(dst, left[0], right[0], start=first, stop=False)
                pe.matmul(dst, left[0], right[1], start=False, stop=False)
                return pe.matmul(dst, left[1], right[0], start=False, stop=last)

            def tile(key, s, rights, c0=0, n=TH, chunks=None):
                b = out(key)
                for k, right in enumerate(rights):
                    ins = mm3(b[:, 0:n], w(s, k, c0), right, k == 0, k == len(rights) - 1)
                filled(ins, key)
                return ins

            def sum_squares(norm, order):
                for f, (c0, c1) in enumerate(HALF):
                    pe.wait_ge(sums, 2 * order + f + 1)
                    key = ("ssq", norm, f)
                    filled(pe.matmul(out(key)[:, 0:TH], ones[:, :], acc[:, c0:c1], start=True, stop=True), key)

            pe.wait_ge(consts_in, 48)
            pe.wait_ge(gains_in, 16 * 8)
            filled(pe.transpose(out(("gain",))[:, 0:NG], gains[0:NG, :], ident[0:NG, 0:NG]), ("gain",))
            pe.wait_ge(x_in, 16 * 5)
            b = out(("xs",))
            for c in range(KD):
                ins = pe.transpose(b[:, c * NB:(c + 1) * NB], x_nat[0:NB, 4, c * P:(c + 1) * P], ident[0:NB, 0:NB])
            filled(ins, ("xs",))
            for c in range(KD):
                b = out(("xt", c))
                for t in range(4):
                    ins = pe.transpose(b[:, t * P:(t + 1) * P], x_nat[:, t, c * P:(c + 1) * P], ident[:, :])
                filled(ins, ("xt", c))
            pe.wait_ge(cp_in, 16)
            b = out(("cp",))
            n = NB * NST
            for g in range(4):
                ins = pe.transpose(b[:, g * n:(g + 1) * n], cp_nat[0:n, g * P:(g + 1) * P], ident[0:n, 0:n])
            filled(ins, ("cp",))
            pe.wait_ge(wuk_in, 16)
            for h in range(NH):
                b = out(("wuk", h))
                for k in (0, 1):
                    ins = pe.transpose(b[:, k * P:(k + 1) * P], wuk_raw[:, k, h * P:(h + 1) * P], ident[:, :])
                filled(ins, ("wuk", h))

            pe.wait_ge(ones_set, 1)
            split(("xs1",))
            for m in range(10):
                weights(S_IN + m)
                for f, (c0, c1) in enumerate(HALF):
                    ins = tile(("in", m, f), S_IN + m, [(B_hi[:, k, c0:c1], B_lo[:, k, c0:c1]) for k in range(KD)])
                if m == 0:
                    sum_squares("n1", 0)
                if m == 6:
                    for f, (c0, c1) in enumerate(HALF):
                        after(("krx", f))
                        filled(pe.matmul(out(("rotk", f))[:, 0:TH], perm[:, :], krx[:, c0:c1], start=True, stop=True), ("rotk", f))
                if m == 7:
                    sum_squares("nq", 1)
                if m == 8:
                    sum_squares("nkv", 2)
            for p, (s, key) in enumerate(((S_UQ, "un"), (S_UQ + 1, "un"), (S_UQ + 2, "ur"))):
                weights(s)
                for i in (0, 1):
                    for f, (c0, c1) in enumerate(HALF):
                        if p == 0 and i == 0:
                            split(("cq", 2, f))
                        ins = tile((key, 2 * p + i if p < 2 else i, f), s,
                                   [(cqg_hi[:, k, c0:c1], cqg_lo[:, k, c0:c1]) for k in range(KQ)], c0=i * P)
            weights(S_POOL)
            for g in range(4):
                split(("pm", g))
                for f, (c0, c1) in enumerate(HALF):
                    key = ("py", g, f)
                    ins = mm3(out(key)[:, 0:TH], w(S_POOL, g), (pm_hi[g][:, c0:c1], pm_lo[g][:, c0:c1]), True, True)
                    filled(ins, key)
                if g < 2:
                    for f, (c0, c1) in enumerate(HALF):
                        after(("qx", g, f))
                        filled(pe.matmul(out(("rotq", g, f))[:, 0:TH], perm[:, :], qx[:, g, c0:c1], start=True, stop=True),
                               ("rotq", g, f))
            for t in range(4):
                b = out(("ct", t))
                for r in (0, 1):
                    ins = pe.transpose(b[:, r * P:(r + 1) * P], cT[:, r, t * P:(t + 1) * P], ident[:, :])
                filled(ins, ("ct", t))
            b = out(("kt",))
            for t in range(4):
                ins = pe.transpose(b[:, t * RP:(t + 1) * RP], kr[0:RP, t * P:(t + 1) * P], ident[0:RP, 0:RP])
            filled(ins, ("kt",))
            b = out(("smp",))
            for r in (0, 1):
                pe.transpose(b[0:NB, r * P:(r + 1) * P], cT[:, r, TP:T], ident[:, :])
            filled(pe.transpose(b[0:NB, KVL:KVL + RP], kr[0:RP, TP:T], ident[0:RP, 0:RP]), ("smp",))
            b = out(("us",))
            for g in range(4):
                ins = pe.transpose(b[0:NB, g * P:(g + 1) * P], up[:, g, NST + TP:NST + T], ident[:, :])
            filled(ins, ("us",))
            b = out(("ut",))
            for g in range(4):
                ins = pe.transpose(b[0:NST, g * P:(g + 1) * P], up[:, g, TP:NST + TP], ident[:, :])
            filled(ins, ("ut",))

            b = out(("qls",))
            for r in (0, 1):
                for h in range(NH):
                    c = (r * NH + h) * NB
                    ins = mm3(b[:, c:c + NB], (wuk_hi[:, h, r * P:(r + 1) * P], wuk_lo[:, h, r * P:(r + 1) * P]),
                              (A_hi[:, h, TP:T], A_lo[:, h, TP:T]), True, True)
            filled(ins, ("qls",))

            def latent_queries(h):
                for r in (0, 1):
                    filled(mm3(out(("ql", h, r)), (wuk_hi[:, h, r * P:(r + 1) * P], wuk_lo[:, h, r * P:(r + 1) * P]),
                               (A_hi[:, h, 0:TP], A_lo[:, h, 0:TP]), True, True), ("ql", h, r))

            def scores(h, i):
                q, n = slice(i * P, (i + 1) * P), (i + 1) * P
                b = out(("s", h, i))[:, 0:n]
                split(("ql", h, 1))
                for r in (0, 1):
                    mm3(b, (ql_hi[:, r, q], ql_lo[:, r, q]), (cT_hi[:, r, 0:n], cT_lo[:, r, 0:n]), r == 0, False)
                filled(mm3(b, (qr_hi[:, h, q], qr_lo[:, h, q]), (kr_hi[:, 0:n], kr_lo[:, 0:n]), False, True), ("s", h, i))

            def values(h):
                split(("pt", h, 3))
                for r in (0, 1):
                    b = out(("pv", h, r))
                    for j in range(4):
                        ins = mm3(b[:, j * P:TP], (cn_hi[:, j, r * P:(r + 1) * P], cn_lo[:, j, r * P:(r + 1) * P]),
                                  (PT_hi[:, j, j * P:TP], PT_lo[:, j, j * P:TP]), j == 0, j == 3)
                    filled(ins, ("pv", h, r))

            def up_values(h):
                split(("pv", h, 1))
                b = out(("uv", h))
                for r in (0, 1):
                    ins = mm3(b, w(S_UV, r, h * P), (ol_hi[:, r, :], ol_lo[:, r, :]), r == 0, r == 1)
                filled(ins, ("uv", h))

            us = units()
            latent_queries(0)
            scores(*us[0])
            scores(*us[1])
            scores(*us[2])
            after(("sprod",))
            filled(pe.matmul(out(("snew",))[0:SQ, 0:1], cols[:, 0].rearrange("p b h -> p (b h)"), ones[:, 0:1],
                             start=True, stop=True), ("snew",))
            weights(S_UV)
            for n, (h, i) in enumerate(us):
                b = out(("pt", h, i))
                after(("pn", h, i))
                for j in range(i + 1):
                    ins = pe.transpose(b[:, j * P:(j + 1) * P], prob[i][:, j * P:(j + 1) * P], ident[:, :])
                filled(ins, ("pt", h, i))
                if n + 3 < len(us):
                    scores(*us[n + 3])
                if i == 0 and h + 1 < NH:
                    latent_queries(h + 1)
                if i == 0 and h:
                    up_values(h - 1)
                if i == 3:
                    values(h)
            up_values(NH - 1)

            b = out(("own",))
            pe.wait_ge(own_set, 2)
            for r in (0, 1):
                ins = pe.transpose(b[0:SQ, r * P:(r + 1) * P], own_c[:, r].rearrange("p b h -> p (b h)"), ident[:, :])
            filled(ins, ("own",))

            pe.wait_ge(q_built, (P // SQ) * (P // SQ + RP // SQ))
            for b in range(NB):
                dst = out(("sc", b))[:, 0:TPP * SQ].rearrange("p (j t) -> p j t", j=TPP)
                after(("turned", b))
                for k in range(NK):
                    x = turned_c[:, b % 2, :, k, :] if k < KVL // SQ else turned_r[:, b % 2, :, k - KVL // SQ, :]
                    ins = pe.matmul(dst, q_diag[:, k].rearrange("p i b h -> p (i b h)"), x, start=(k == 0), stop=(k == NK - 1))
                filled(ins, ("sc", b))
            after(("own_p",))
            freed(pe, ("own",))
            pe.matmul(accO[0:SQ, 0:KVL], diag[0:SQ, :], own_nat[0:SQ, :], start=True, stop=False)
            after(("spread_p",))
            for b in range(NB):
                for j in range(TPP):
                    c = b * TPP * SQ + j * SQ
                    ins = pe.matmul(accO[0:SQ, 0:KVL], P_pad[:, c:c + SQ], past_c[b][:, j, :],
                                    start=False, stop=(b == NB - 1 and j == TPP - 1))
            ins.then_inc(past_mixed, 1)
            b = out(("ot",))
            after(("rows",))
            for r in (0, 1):
                ins = pe.transpose(b[:, r * SQ:(r + 1) * SQ], o_rows[0:SQ, r * P:(r + 1) * P], ident[0:SQ, 0:SQ])
            filled(ins, ("ot",))

            def softmax_sums(mxt, mx, mxb, dg, tot, total):
                b = out(mxt)
                after(mx)
                filled(pe.transpose(b[0:NB * NH, 0:P], cols[:, 3].rearrange("p b h -> p (b h)"), ident[:, :]), mxt)
                b = out(mxb)
                after(dg)
                filled(pe.matmul(b[:, 0:NB * NH], ones[0:NB * NH, :], diag[0:NB * NH, :], start=True, stop=True), mxb)
                b = out(tot)
                after(total)
                filled(pe.matmul(b[:, 0:NB * NH], ones[:, :], cols[:, 6].rearrange("p b h -> p (b h)"), start=True, stop=True), tot)

            split(("ot",))
            b = out(("uvs",))
            for h in range(NH):
                for r in (0, 1):
                    ins = mm3(b[:, h * NB:(h + 1) * NB], w(S_UV, r, h * P), (ols_hi[:, r, h, :], ols_lo[:, r, h, :]), r == 0, r == 1)
            filled(ins, ("uvs",))

            split(("uvs",))
            A = lambda c0, c1: [(A_hi[:, k, c0:c1], A_lo[:, k, c0:c1]) for k in range(KD)]
            B = lambda c0, c1: [(B_hi[:, k, c0:c1], B_lo[:, k, c0:c1]) for k in range(KD)]
            for m in range(KD):
                weights(S_OUT + m)
                for f, (c0, c1) in enumerate(HALF):
                    ins = tile(("o", m, f), S_OUT + m, A(c0, c1))
                if m == 1:
                    after(("memn",))
                    for k in range(4):
                        b = out(("mt", k))
                        for c in (0, 1):
                            for t in (0, 1):
                                ins = pe.transpose(b[:, (2 * c + t) * P:(2 * c + t + 1) * P],
                                                   m_nat[:, t, (2 * k + c) * P:(2 * k + c + 1) * P], ident[:, :])
                        filled(ins, ("mt", k))
            def rows(n):
                b = out(("mn", n))
                for i in (0, 1):
                    freed(pe, ("mm", 2 * n + i))
                    for t in (0, 1):
                        ins = pe.transpose(b[:, (2 * t + i) * P:(2 * t + i + 1) * P],
                                           kv_T[:, (2 * n + i) % 4, t * P:(t + 1) * P], ident[:, :])
                filled(ins, ("mn", n))

            for j in range(16):
                weights(S_MK + j)
                tile(("mm", j), S_MK + j, [(mT_hi[:, k, :], mT_lo[:, k, :]) for k in range(KD)], n=NMEM)
                if j >= 2 and j % 2 == 0:
                    rows(j // 2 - 1)
            rows(7)
            for m in range(KD):
                weights(S_XQ + m)
                for f, (c0, c1) in enumerate(HALF):
                    if m == 0:
                        split(("xo1", KD - 1, f))
                    ins = tile(("xq", m, f), S_XQ + m, B(c0, c1))
                if m == 0:
                    sum_squares("nx", 3)
            pe.wait_ge(qcs_set, KD)
            for k in (0, 1):
                b = out(("qt", k))
                for c in range(4):
                    ins = pe.transpose(b[0:NB, c * P:(c + 1) * P], qcs[:, 4 * k + c, :], ident[:, :])
                filled(ins, ("qt", k))

            def mem_scores(h):
                for ip in (0, 1):
                    b = out(("cs", h, ip))
                    for i in (0, 1):
                        q = slice((2 * ip + i) * P, (2 * ip + i + 1) * P)
                        for dc in (0, 1):
                            c = 2 * h + dc
                            ins = mm3(b[:, i * NMEM:(i + 1) * NMEM], (q_hi[:, c, q], q_lo[:, c, q]),
                                      (mkT_hi[:, c, :], mkT_lo[:, c, :]), dc == 0, dc == 1)
                    filled(ins, ("cs", h, ip))

            def spread(b):
                for k in (0, 1):
                    freed(pe, ("qt", k))
                    key = ("qb", b, k)
                    filled(pe.matmul(out(key), ident[0:NB, b:b + 1].to_broadcast([NB, P]), q_nat[0:NB, k * 512:(k + 1) * 512],
                                     start=True, stop=True), key)

            split(("xq", KD - 1, 1))
            split(("mn", 7))
            mem_scores(0)
            for h in range(NH):
                if h + 1 < NH:
                    mem_scores(h + 1)
                after(("cpn", h))
                for mb in (0, 1):
                    b = out(("cpt", h, mb))
                    for i in range(4):
                        ins = pe.transpose(b[:, i * P:(i + 1) * P], Pc[:, h % 2, i // 2, i % 2, mb * P:(mb + 1) * P], ident[:, :])
                    filled(ins, ("cpt", h, mb))
                spread(2 * h)
                split(("cpt", h, 1))
                for dc in (0, 1):
                    b = out(("cpv", h, dc))
                    c = 2 * h + dc
                    for mb in (0, 1):
                        ins = mm3(b, (mvn_hi[:, mb, c * P:(c + 1) * P], mvn_lo[:, mb, c * P:(c + 1) * P]),
                                  (PTc_hi[:, mb, :], PTc_lo[:, mb, :]), mb == 0, mb == 1)
                    filled(ins, ("cpv", h, dc))
                spread(2 * h + 1)
            softmax_sums(("cmxt",), ("cmx",), ("cmxb",), ("cdiag",), ("ctot",), ("csum",))
            after(("cpnorm",))
            for b in range(NB):
                n = NB + b
                pe.wait_ge(kv_in[n % K3], 16 * (n // K3 + 1))
                for c in range(KD):
                    for m2 in (0, 1):
                        ins = pe.matmul(accO[:, c * NB + b:c * NB + b + 1], kv_ring[:, n % K3, m2, c * P:(c + 1) * P],
                                        Pcs[:, b, m2, c // 2:c // 2 + 1], start=(b == 0 and c == 0 and m2 == 0),
                                        stop=(b == NB - 1 and c == KD - 1 and m2 == 1), skip_group_check=True)
                ins.then_inc(v_used, 1)
            split(("co",))
            for m in range(KD):
                weights(S_XO + m)
                for f, (c0, c1) in enumerate(HALF):
                    ins = tile(("xo", m, f), S_XO + m, A(c0, c1))
            for j in range(NF):
                for i, key in enumerate(("g", "u")):
                    s = S_FFN + 2 * j + i
                    weights(s)
                    for f, (c0, c1) in enumerate(HALF):
                        if j == 0 and i == 0:
                            split(("xo2", KD - 1, f))
                        ins = tile((key, j, f), s, B(c0, c1))
                if j == 0:
                    sum_squares("nf", 4)
            for m in range(KD):
                b = [out(("d", m, f)) for f in (0, 1)]
                for part, (k0, k1) in enumerate(DPART):
                    s = S_DOWN + 3 * m + part
                    weights(s)
                    for f, (c0, c1) in enumerate(HALF):
                        if m == 0 and part == 2:
                            split(("h", NF - 1, f))
                        elif m == 0:
                            split(("h", k1 - 1, f))
                        for k in range(k0, k1):
                            ins = mm3(b[f][:, 0:TH], w(s, k - k0), (h_hi[:, k, c0:c1], h_lo[:, k, c0:c1]), k == 0, k == NF - 1)
                        if part == 2:
                            filled(ins, ("d", m, f))
                    if part < 2:
                        ins.then_inc(down_used, 1)
            sum_squares("nz", 5)
            for t in range(5):
                n = P if t < 4 else NB
                c = t * P
                after(("yT", KD - 1, 0 if c + n <= TH else 1))
                for k in (0, 1):
                    b = out(("y", t, k))
                    for i in range(4):
                        ins = pe.transpose(b[0:n, i * P:(i + 1) * P], yT[:, 4 * k + i, c:c + n], ident[:, :])
                    filled(ins, ("y", t, k))
            assert uses[0] == len(BANK.at)


_INS = ["x_prompt", "x_sample", "mem_prompt", "cache_kv_latent", "cache_k_rope", "cache_pool", "cache_mem_k",
        "cache_mem_v", "page_table", "norm_mix", "w_in", "q_norm", "w_uq", "kv_norm", "w_uk", "w_uv", "w_pool",
        "pool_scale", "w_out", "norm_x", "mem_norm", "w_xq", "w_mk", "w_mv", "w_xo", "norm_ffn", "w_gate", "w_up",
        "w_down", "norm_final"]
_OUTS = [(1, TP, D), (NB, 1, D), (1, 1, TP, KVL), (1, 1, TP, RP), (1, 1, NST, PW), (1, 1, NMEM, NH, MD),
         (1, 1, NMEM, NH, MD), (1, NB, 1, KVL), (1, NB, 1, RP), (1, NB, NST, PW)]


def constants():
    f = np.float32
    perm = np.zeros((P, P), f)
    for m in range(P):
        perm[m ^ 32, m] = 1
    q, k = np.meshgrid(np.arange(P), np.arange(P), indexing="ij")
    mask = np.where(k <= q, f(0), f(BIG))
    half = RP // 2
    inv = np.power(f(10000.0), -(np.arange(half, dtype=f) / f(half))).astype(f)
    pos = np.concatenate([np.arange(TP), np.full(NB, PAGE * NPG)]).astype(f)
    ang = (inv[:, None] * pos[None, :]).astype(f)
    cos, sin = np.cos(ang).astype(f), np.sin(ang).astype(f)
    rcnt = np.ones((4, 16), f)
    for g, win in enumerate(WINDOWS):
        rcnt[g] = f(1) / np.minimum(win, np.arange(16) + 1).astype(f)
    rcnt = np.broadcast_to(rcnt.reshape(1, 64), (P, 64))
    row = (np.arange(P) % (PAGE // TPP)).astype(f)[:, None]
    is_sample = (np.arange(P)[:, None] % (NB * NH) // NH == np.arange(NB)).astype(f)
    return np.ascontiguousarray(np.concatenate(
        [np.eye(P, dtype=f), perm, mask, np.concatenate([cos] * 4), np.concatenate([-sin, sin] * 2), rcnt, row, is_sample], 1, dtype=f))


def kernel(**inputs):
    import concourse.bacc as _bacc
    from concourse.bass_utils import run_bass_kernel_spmd as _run

    nc = _bacc.Bacc("TRN2", target_bir_lowering=False, num_devices=1)
    arrays, aps = {}, {}
    for name in _INS:
        x = np.ascontiguousarray(inputs[name])
        arrays[f"in_{name}_dram"] = x
        aps[name] = nc.dram_tensor(f"in_{name}_dram", x.shape, mybir.dt.from_np(x.dtype), kind="ExternalInput").ap()
    table = constants()
    arrays["in_consts_dram"] = table
    consts = nc.dram_tensor("in_consts_dram", table.shape, F32, kind="ExternalInput").ap()
    outs = [nc.dram_tensor(f"out_{i}_dram", shape, F32, kind="ExternalOutput").ap() for i, shape in enumerate(_OUTS)]
    build(nc, aps, consts, outs)
    r = _run(nc, [arrays], core_ids=[0])
    return tuple(r.results[0][f"out_{i}_dram"] for i in range(len(_OUTS)))
```
